# Optimizing a Trainium2 kernel written in Bass

```python
import math
import jax, jax.numpy as jnp
from jax import lax
import numpy as np

D_MODEL = 1024
BATCH = 1
SEQ = 256
DEPTH = 2

GRID_W = 64
CTX_LEN = 256
N_MOD = 6
NORM_EPS = 1e-6
ROPE_BASE = 10000.0
Q_BLOCK = 128
MLA_HEADS = 8
MLA_HEAD_DIM = D_MODEL // 16
MLA_ROPE_DIM = D_MODEL // 32
MLA_Q_RANK = 3 * D_MODEL // 8
MLA_KV_RANK = D_MODEL // 4
MLA_W = MLA_HEADS * MLA_HEAD_DIM
DIFF_HEADS = 4
DIFF_HEAD_DIM = D_MODEL // 16
DIFF_W = DIFF_HEADS * 2 * DIFF_HEAD_DIM
MIX_W = MLA_W + DIFF_W
IN_SIZES = (MLA_Q_RANK, MLA_KV_RANK, MLA_ROPE_DIM, DIFF_W, DIFF_W, DIFF_W)
IN_SPLITS = (384, 640, 672, 1184, 1696)
PROJ_W = 2208
PEER_HEADS = 8
PEER_TOPK = 16
N_KEYS = 128
N_EXPERTS = N_KEYS * N_KEYS
PEER_KEY_DIM = D_MODEL // 4
PEER_KEY_HALF = PEER_KEY_DIM // 2
PEER_CHUNK = 128

kernel_name = 'hybrid_mla_diffattn_peer_dit'

def rmsnorm(x, g):
    x32 = x.astype(jnp.float32)
    y = x32 * lax.rsqrt(jnp.mean(x32 * x32, axis=-1, keepdims=True) + NORM_EPS)
    return y.astype(x.dtype) * g

def axial_angles(row, col, dim):
    quarter = dim // 4
    inv_freq = ROPE_BASE ** (-jnp.arange(quarter, dtype=jnp.float32) / quarter)
    return jnp.concatenate([row[:, None] * inv_freq, col[:, None] * inv_freq], axis=-1)

def apply_rope(x, ang):
    cos = jnp.cos(ang).astype(x.dtype)
    sin = jnp.sin(ang).astype(x.dtype)
    x1, x2 = x[..., 0::2], x[..., 1::2]
    return jnp.stack([x1 * cos - x2 * sin, x1 * sin + x2 * cos], axis=-1).reshape(x.shape)

def sweep_query_blocks(fn, q):
    B, S = q.shape[:2]
    nb = S // Q_BLOCK
    qb = jnp.moveaxis(q.reshape((B, nb, Q_BLOCK) + q.shape[2:]), 1, 0)
    out = lax.map(fn, qb)
    return jnp.moveaxis(out, 0, 1).reshape((B, S) + out.shape[3:])

def softmax_attend(q, k, v):
    s = jnp.einsum('bqhd,bkhd->bhqk', q, k).astype(jnp.float32) * (q.shape[-1] ** -0.5)
    p = jax.nn.softmax(s, axis=-1)
    return jnp.einsum('bhqk,bkhd->bqhd', p.astype(v.dtype), v)

def diff_attend(q, k, v, lam):
    s = jnp.einsum('bqhcd,bkhcd->bhcqk', q, k).astype(jnp.float32) * (q.shape[-1] ** -0.5)
    p = jax.nn.softmax(s, axis=-1)
    a = p[:, :, 0] - lam * p[:, :, 1]
    return jnp.einsum('bhqk,bkhd->bqhd', a.astype(v.dtype), v)

def mla_qkv(cq, ckv, kr, p, ang):
    B, L = cq.shape[:2]
    cq = rmsnorm(cq, p['mla_q_norm_g'])
    q_nope = (cq @ p['mla_wq_up']).reshape(B, L, MLA_HEADS, MLA_HEAD_DIM)
    q_rope = (cq @ p['mla_wq_rope']).reshape(B, L, MLA_HEADS, MLA_ROPE_DIM)
    ckv = rmsnorm(ckv, p['mla_kv_norm_g'])
    k_nope = (ckv @ p['mla_wk_up']).reshape(B, L, MLA_HEADS, MLA_HEAD_DIM)
    v = (ckv @ p['mla_wv_up']).reshape(B, L, MLA_HEADS, MLA_HEAD_DIM)
    if ang is not None:
        q_rope = apply_rope(q_rope, ang[:, None, :])
        kr = apply_rope(kr, ang)
    k_rope = jnp.broadcast_to(kr[:, :, None, :], (B, L, MLA_HEADS, MLA_ROPE_DIM))
    return (jnp.concatenate([q_nope, q_rope], axis=-1),
            jnp.concatenate([k_nope, k_rope], axis=-1), v)

def diff_qkv(q, k, v, ang):
    B, L = q.shape[:2]
    q = q.reshape(B, L, DIFF_HEADS, 2, DIFF_HEAD_DIM)
    k = k.reshape(B, L, DIFF_HEADS, 2, DIFF_HEAD_DIM)
    v = v.reshape(B, L, DIFF_HEADS, 2 * DIFF_HEAD_DIM)
    if ang is not None:
        q = apply_rope(q, ang[:, None, None, :])
        k = apply_rope(k, ang[:, None, None, :])
    return q, k, v

def merge_groups(o_mla, o_diff, p, lam_init):
    B, L = o_mla.shape[:2]
    o_diff = rmsnorm(o_diff, p['diff_subnorm_g']) * (1.0 - lam_init)
    cat = jnp.concatenate([o_mla.reshape(B, L, MLA_W), o_diff.reshape(B, L, DIFF_W)], axis=-1)
    return cat @ p['w_out']

def parallel_mixers(h, hc, p, ang_mla, ang_diff, lam, lam_init, need_ctx_out):
    parts = jnp.split(h @ p['w_in'], IN_SPLITS, axis=-1)
    parts_c = jnp.split(hc @ p['w_in'], IN_SPLITS, axis=-1)
    q_m, k_m, v_m = mla_qkv(parts[0], parts[1], parts[2], p, ang_mla)
    qc_m, kc_m, vc_m = mla_qkv(parts_c[0], parts_c[1], parts_c[2], p, None)
    q_d, k_d, v_d = diff_qkv(parts[3], parts[4], parts[5], ang_diff)
    qc_d, kc_d, vc_d = diff_qkv(parts_c[3], parts_c[4], parts_c[5], None)
    k_m_all = jnp.concatenate([kc_m, k_m], axis=1)
    v_m_all = jnp.concatenate([vc_m, v_m], axis=1)
    k_d_all = jnp.concatenate([kc_d, k_d], axis=1)
    v_d_all = jnp.concatenate([vc_d, v_d], axis=1)
    o_m = sweep_query_blocks(lambda qb: softmax_attend(qb, k_m_all, v_m_all), q_m)
    o_d = sweep_query_blocks(lambda qb: diff_attend(qb, k_d_all, v_d_all, lam), q_d)
    y = merge_groups(o_m, o_d, p, lam_init)
    yc = None
    if need_ctx_out:
        yc = merge_groups(softmax_attend(qc_m, kc_m, vc_m),
                          diff_attend(qc_d, kc_d, vc_d, lam), p, lam_init)
    return y, yc

def peer_ffn(h, p):
    B, L, D = h.shape
    T = B * L

    def expert_block(xb):
        q = (xb @ p['peer_wq']).reshape(PEER_CHUNK, PEER_HEADS, 2, PEER_KEY_HALF)
        s = jnp.einsum('thcd,ckd->thck', q, p['peer_subkeys']).astype(jnp.float32)
        sv, si = lax.top_k(s, PEER_TOPK)
        n_cand = PEER_TOPK * PEER_TOPK
        cand_s = (sv[:, :, 0, :, None] + sv[:, :, 1, None, :]).reshape(PEER_CHUNK, PEER_HEADS, n_cand)
        cand_i = (si[:, :, 0, :, None] * N_KEYS + si[:, :, 1, None, :]).reshape(PEER_CHUNK, PEER_HEADS, n_cand)
        top_s, pos = lax.top_k(cand_s, PEER_TOPK)
        eidx = jnp.take_along_axis(cand_i, pos, axis=-1).reshape(PEER_CHUNK, PEER_HEADS * PEER_TOPK)
        gate = jax.nn.softmax(top_s, axis=-1).reshape(PEER_CHUNK, PEER_HEADS * PEER_TOPK).astype(xb.dtype)
        u = jnp.take(p['peer_u'], eidx, axis=0)
        v = jnp.take(p['peer_v'], eidx, axis=0)
        act = jax.nn.gelu(jnp.einsum('ted,td->te', u, xb), approximate=False) * gate
        return jnp.einsum('te,ted->td', act, v)

    out = lax.map(expert_block, h.reshape(T // PEER_CHUNK, PEER_CHUNK, D))
    return out.reshape(B, L, D)

def setup_inputs(seed: int = 0) -> dict:
    key = jax.random.key(seed)
    ks = jax.random.split(key, 23)
    nrm = jax.random.normal
    f32 = jnp.float32
    L, D = DEPTH, D_MODEL

    def w(k, shape, fan_in):
        return nrm(k, shape, f32) * (fan_in ** -0.5)

    def gain(k, shape):
        return 1.0 + 0.02 * nrm(k, shape, f32)

    return dict(
        x=nrm(ks[0], (BATCH, SEQ, D), f32),
        c=nrm(ks[1], (BATCH, D), f32),
        ctx=nrm(ks[2], (BATCH, CTX_LEN, D), f32),
        c_ctx=nrm(ks[3], (D,), f32),
        norm_attn_g=gain(ks[4], (L, D)),
        norm_ffn_g=gain(ks[5], (L, D)),
        w_ada=0.5 * w(ks[6], (L, D, N_MOD * D), D),
        b_ada=0.01 * nrm(ks[7], (L, N_MOD * D), f32),
        w_in=w(ks[8], (L, D, PROJ_W), D),
        mla_q_norm_g=gain(ks[9], (L, MLA_Q_RANK)),
        mla_wq_up=w(ks[10], (L, MLA_Q_RANK, MLA_HEADS * MLA_HEAD_DIM), MLA_Q_RANK),
        mla_wq_rope=w(ks[11], (L, MLA_Q_RANK, MLA_HEADS * MLA_ROPE_DIM), MLA_Q_RANK),
        mla_kv_norm_g=gain(ks[12], (L, MLA_KV_RANK)),
        mla_wk_up=w(ks[13], (L, MLA_KV_RANK, MLA_W), MLA_KV_RANK),
        mla_wv_up=w(ks[14], (L, MLA_KV_RANK, MLA_W), MLA_KV_RANK),
        diff_lambda=0.1 * nrm(ks[15], (L, 4, DIFF_HEAD_DIM), f32),
        diff_subnorm_g=gain(ks[16], (L, 2 * DIFF_HEAD_DIM)),
        w_out=w(ks[17], (L, MIX_W, D), MIX_W),
        peer_wq=w(ks[18], (L, D, PEER_HEADS * PEER_KEY_DIM), D),
        peer_subkeys=w(ks[19], (L, 2, N_KEYS, PEER_KEY_HALF), PEER_KEY_HALF),
        peer_u=w(ks[20], (L, N_EXPERTS, D), D),
        peer_v=0.5 * nrm(ks[21], (L, N_EXPERTS, D), f32),
        final_norm_g=gain(ks[22], (D,)),
    )

def reference(x, c, ctx, c_ctx, norm_attn_g, norm_ffn_g, w_ada, b_ada, w_in,
              mla_q_norm_g, mla_wq_up, mla_wq_rope, mla_kv_norm_g, mla_wk_up, mla_wv_up,
              diff_lambda, diff_subnorm_g, w_out, peer_wq, peer_subkeys, peer_u, peer_v,
              final_norm_g):
    S = x.shape[1]
    ROWS = S // GRID_W
    row = jnp.repeat(jnp.arange(ROWS, dtype=jnp.float32), GRID_W)
    col = jnp.tile(jnp.arange(GRID_W, dtype=jnp.float32), ROWS)
    ang_mla = axial_angles(row, col, MLA_ROPE_DIM)
    ang_diff = axial_angles(row, col, DIFF_HEAD_DIM)
    s_c = jax.nn.silu(c)
    s_cc = jax.nn.silu(c_ctx)
    xc = ctx
    for l in range(DEPTH):
        last = l == DEPTH - 1
        p = dict(w_in=w_in[l], mla_q_norm_g=mla_q_norm_g[l], mla_wq_up=mla_wq_up[l],
                 mla_wq_rope=mla_wq_rope[l], mla_kv_norm_g=mla_kv_norm_g[l],
                 mla_wk_up=mla_wk_up[l], mla_wv_up=mla_wv_up[l],
                 diff_subnorm_g=diff_subnorm_g[l], w_out=w_out[l], peer_wq=peer_wq[l],
                 peer_subkeys=peer_subkeys[l], peer_u=peer_u[l], peer_v=peer_v[l])
        sh1, sc1, g1, sh2, sc2, g2 = jnp.split((s_c @ w_ada[l] + b_ada[l])[:, None, :], N_MOD, axis=-1)
        sh1c, sc1c, g1c, sh2c, sc2c, g2c = jnp.split(s_cc @ w_ada[l] + b_ada[l], N_MOD, axis=-1)
        lam_init = 0.8 - 0.6 * math.exp(-0.3 * l)
        dl = diff_lambda[l].astype(jnp.float32)
        lam = jnp.exp(jnp.sum(dl[0] * dl[1])) - jnp.exp(jnp.sum(dl[2] * dl[3])) + lam_init
        h = rmsnorm(x, norm_attn_g[l]) * (1 + sc1) + sh1
        hc = rmsnorm(xc, norm_attn_g[l]) * (1 + sc1c) + sh1c
        y, yc = parallel_mixers(h, hc, p, ang_mla, ang_diff, lam, lam_init, not last)
        x = x + g1 * y
        h = rmsnorm(x, norm_ffn_g[l]) * (1 + sc2) + sh2
        x = x + g2 * peer_ffn(h, p)
        if not last:
            xc = xc + g1c * yc
            hc = rmsnorm(xc, norm_ffn_g[l]) * (1 + sc2c) + sh2c
            xc = xc + g2c * peer_ffn(hc, p)
    return rmsnorm(x, final_norm_g)


_drawn_inputs = setup_inputs


def setup_inputs(seed=0):
    import zlib

    import numpy as np

    out = dict(_drawn_inputs(seed))
    spreads = {}
    factors = {'norm_attn_g': 6.419,
     'norm_ffn_g': 3.151,
     'b_ada': 2.713,
     'mla_q_norm_g': 8.0,
     'mla_wq_rope': 2.784,
     'mla_kv_norm_g': 8.0,
     'diff_lambda': 6.64,
     'diff_subnorm_g': 5.899,
     'final_norm_g': 2.818}
    for name, (base, spread) in spreads.items():
        noise = np.random.default_rng([zlib.crc32(name.encode()), seed]).standard_normal(out[name].shape)
        drawn = base * np.exp(spread * noise) if base else spread * noise
        out[name] = __import__('jax').numpy.asarray(drawn.astype(out[name].dtype))
    for name, factor in factors.items():
        out[name] = (out[name] * factor).astype(out[name].dtype)
    return out
```

```python
import math
from contextlib import ExitStack

import concourse.bass as bass
from concourse import mybir

F32 = mybir.dt.float32
U32 = mybir.dt.uint32
ALU = mybir.AluOpType
ACT = mybir.ActivationFunctionType
AX_X = mybir.AxisListType.X

P = 128
D = 1024
KD = D // P
DEPTH = 2
TILES = 4
EPS = 1e-6
QR, KVR, RD = 384, 256, 32
MH, MD = 8, 64
MQ = MD + RD
DH, DD = 4, 64
PH, TOPK, NK = 8, 16, 128
SLOTS = PH * TOPK
W = 512
NA = 3
NB = 3
WSLOTS = 2
RING = 8
HB = 3
UNIT = 8
UNITS = SLOTS // UNIT
CTX, LAT = 0, 1
CHUNKS = {"cq": (0, 384), "kv": (384, 288), "qd": (672, 512), "kd": (1184, 512), "vd": (1696, 512)}
SC_M = MQ ** -0.5
SC_D = DD ** -0.5
LOWEST = -3.0e38

R_C, R_CC, R_NA, R_NF, R_QN, R_KN, R_SN = 0, 8, 16, 32, 48, 54, 58
ROWS = 60
MODS = 6 * KD


def lam_init(l):
    return 0.8 - 0.6 * math.exp(-0.3 * l)


def blocks_of(l, g):
    return [4 * l + 2 * g - (2 if l else 0) + t for t in range(2)]


def block_home(b):
    return (0, b) if b < 4 else (1, b - 2)


def front(l, g):
    full = not (l == DEPTH - 1 and g == CTX)
    out = [("norm1", l, g, t) for t in range(2)]
    names = (["qd"] if full else []) + ["kd", "vd"] + (["cq"] if full else []) + ["kv"]
    prior = None
    for n in names:
        out.append(("in", l, g, n))
        if prior and prior != "vd":
            out.append(("turn", l, g, prior))
        prior = n
    out.append(("turn", l, g, "kv"))
    if full:
        out += [("up", l, g, "q"), ("up", l, g, "k"), ("turn", l, g, "q"), ("up", l, g, "v"), ("turn", l, g, "k")]
    else:
        out += [("up", l, g, "k"), ("up", l, g, "v"), ("turn", l, g, "k")]
    return out


def middle(l, g):
    out = []
    for t in range(2):
        out += [("attn", l, g, t, i) for i in range(-1, MH + DH + 1)]
        out.append(("heads", l, g, t))
    out += [("out", l, g, n) for n in range(2)]
    out += [("norm2", l, g, t) for t in range(2)]
    return out


def pick(l, g):
    return [("pick", l, g, h) for h in range(PH + 1)]


def weave(background, stream):
    out, at = [], 0
    for n, s in enumerate(background):
        out.append(s)
        to = (n + 1) * len(stream) // len(background)
        out += stream[at:to]
        at = to
    return out


def spans(plan):
    out = []
    for s in plan:
        if s[0] == "units" and out and out[-1][0] == "units" and out[-1][1] == s[1] and out[-1][3] == s[2]:
            out[-1] = ("units", s[1], out[-1][2], s[3])
        else:
            out.append(s)
    return out


def stream_of(b, first=0):
    return [("units", b, u, u + 1) for u in range(first, UNITS)] + [("close", b)]


def make_plan():
    plan = [("consts",)]
    plan += [("ada", 0, n) for n in range(MODS // 4 + 1)] + [("mod", 0)]
    plan += front(0, CTX) + middle(0, CTX)
    picks = pick(0, CTX)
    plan += [picks[0]] + weave(picks[1:], [("units", 0, u, u + 1) for u in range(8)])
    plan += weave(front(0, LAT) + middle(0, LAT) + pick(0, LAT), stream_of(0, 8) + stream_of(1))
    plan += weave([("ada", 1, n) for n in range(MODS // 4 + 1)] + [("mod", 1)] + front(1, CTX), stream_of(2) + stream_of(3))
    plan += front(1, LAT) + middle(1, LAT)
    picks = pick(1, LAT)
    plan += [picks[0]] + weave(picks[1:], [("units", 4, u, u + 1) for u in range(8)])
    plan += stream_of(4, 8) + [("last", 0)] + stream_of(5) + [("last", 1)]
    at = {s: n for n, s in enumerate(plan)}
    for b in range(HB, 6):
        l, tile = block_home(b)
        assert at["close", b - HB] < at["norm2", l, tile // 2, tile % 2], "the inputs of block b - 3 are still in use"
    return spans(plan)


PLAN = make_plan()


FINAL_GAIN_AFTER = sum(s[0] in ("norm1", "norm2") for s in PLAN)


def parts_of(u0, u1):
    out, u = [], u0
    while u < u1:
        m = (u1 - u) // 2 * 2
        if u % 2 == 0 and u > 0 and m >= 4:
            out.append(("loop", u, u + m))
            u += m
        else:
            out.append(("one", u, u + 1))
            u += 1
    return out


def tmp_slot(stage):
    return {"qd": 0, "kd": 2, "cq": 0, "kv": 2}[stage[3]]


def gu(b, u):
    return b * UNITS + u


class Ring:

    def __init__(self, banks):
        self.banks, self.n = banks, 0

    def next(self):
        self.n += 1
        return self.banks[(self.n - 1) % len(self.banks)], self.n


class Ticks:

    def __init__(self):
        self.n = {}

    def __call__(self, name):
        self.n[name] = self.n.get(name, 0) + 1
        return self.n[name]

    def so_far(self, name):
        return self.n.get(name, 0)


def backbone(nc, a, out):
    ctx = ExitStack()
    with ctx:
        def sb(name, shape, dt=F32):
            return ctx.enter_context(nc.sbuf_tensor(name, shape, dt))

        def sem(name):
            return ctx.enter_context(nc.semaphore(name))

        X = sb("X", [P, TILES, D])
        H2 = sb("H2", [P, HB, D])
        HT = sb("HT", [P, KD, 2 * P])
        KTM = sb("KTM", [MQ, MH, TILES * P])
        VM = sb("VM", [P, TILES, MH * MD])
        KTD = sb("KTD", [P, DH, TILES * P])
        VD = sb("VD", [P, TILES, DH * 2 * DD])
        QTM = sb("QTM", [MQ, MH, 2 * P])
        QTD = sb("QTD", [P, DH, 2 * P])
        EXPERT = sb("EXPERT", [P, RING, 2 * D])
        WT = sb("WT", [P, WSLOTS, 4, W])
        SCR = sb("SCR", [P, 4096])
        ACC = sb("ACC", [P, D])
        IDX = sb("IDX", [P, HB, SLOTS], U32)
        GATE = sb("GATE", [P, HB, SLOTS])
        FIX = sb("FIX", [P, 2, UNIT], U32)
        IDN = sb("IDN", [P, P])
        ONES = sb("ONES", [P, P])
        GD = sb("GD", [P, 4, P])
        DIAG = sb("DIAG", [P, 2, 2, P])
        COL = sb("COL", [P, 2, 2 * MODS])
        ST = sb("ST", [P, 2, KD])
        MROW = sb("MROW", [2, 2, W])
        MOD = sb("MOD", [P, DEPTH, MODS, 2])
        SKT = sb("SKT", [P, DEPTH * 2, P])
        LS = sb("LS", [P, 2 * DEPTH])
        LE = sb("LE", [P, 2 * DEPTH])
        LAM = sb("LAM", [P, DEPTH])
        SUBG = sb("SUBG", [P, DEPTH])
        ROPM = sb("ROPM", [P, 2, 2, RD])
        ROPD = sb("ROPD", [P, 2, 2, DD])
        IOTA = sb("IOTA", [P, TOPK])
        EPST = sb("EPST", [P, 1])
        KR = sb("KR", [P, 2, RD])
        SS = sb("SS", [P, 4])
        SQ = sb("SQ", [P, 4])
        RS = sb("RS", [P, 4])
        NS = sb("NS", [P, 1])
        NQ = sb("NQ", [P, 1])
        NR = sb("NR", [P, 1])
        MX = sb("MX", [P, 2, 2])
        NM = sb("NM", [P, 2, 2])
        SUM = sb("SUM", [P, 2, 2])
        INV = sb("INV", [P, 2, 2])
        SV = sb("SV", [P, 2, TOPK])
        SI = sb("SI", [P, 2, TOPK], U32)
        SIF = sb("SIF", [P, 2, TOPK])
        TS = sb("TS", [P, 2, TOPK])
        POS = sb("POS", [P, TOPK], U32)
        AB = sb("AB", [P, 2, TOPK], U32)
        ABF = sb("ABF", [P, 2, TOPK])
        PICK = sb("PICK", [P, 2, TOPK])
        TE = sb("TE", [P, 2, TOPK])
        NT = sb("NT", [P, 2])
        TSUM = sb("TSUM", [P, 2])
        TINV = sb("TINV", [P, 2])
        DOT = sb("DOT", [P, 2, 4])
        GEL = sb("GEL", [P, 2, 4])
        WEI = sb("WEI", [P, 2, 4])

        SK = SCR[:, 0:DEPTH * 2 * P].rearrange("p (i n) -> p i n", n=P)
        LM = SCR[:, 512:1024].rearrange("p (l f n) -> p l f n", l=DEPTH, f=4)
        ROW = SCR[0:ROWS, 1024:1024 + P]
        BROW = SCR[0:2 * MODS, 1536:1536 + P]
        LT = SCR[:, 2048:2048 + 2 * DEPTH * DD].rearrange("p (i n) -> p i n", n=DD)
        XN = SCR[:, 0:D]
        ROT = SCR[:, 0:W]
        TMP = SCR[:, D:D + 4 * W].rearrange("p (s n) -> p s n", s=4)
        ASM = SCR[:, D:4096].rearrange("p (s h n) -> p s h n", s=4, h=MH)
        PR = SCR[:, 0:2048].rearrange("p (r c n) -> p r c n", r=2, c=2)
        PT = SCR[:, 2048:3072].rearrange("p (r n) -> p r n", r=2)
        O = SCR[:, 3072:4096]
        YT = SCR[:, D:D + 2 * W].rearrange("p (s n) -> p s n", s=2)
        GROW = SCR[:, D + 2 * W:D + 3 * W]
        WK = SCR[:, D:D + 256].rearrange("p (c n) -> p c n", c=2)
        CAND = SCR[:, D + 256:D + 512]
        CANW = SCR[:, D + 512:D + 768]
        HOT = SCR[:, D + 1024:D + 1536].rearrange("p (c s n) -> p c s n", c=2, s=TOPK)
        QP = SCR[:, 3072:4096].rearrange("p (r c n) -> p r c n", r=2, c=2)

        banks_a = [ctx.enter_context(nc.psum_tensor(f"PA{i}", [P, W], F32)) for i in range(NA)]
        banks_b = [ctx.enter_context(nc.psum_tensor(f"PB{i}", [P, W], F32)) for i in range(NB)]
        VSUM = [ctx.enter_context(nc.psum_tensor(f"VS{i}", [P, W], F32)) for i in range(2)]

        consts_in = sem("consts_in")
        x_in = sem("x_in")
        fg_in = sem("fg_in")
        piece_in = [sem(f"piece_in{i}") for i in range(WSLOTS)]
        piece_used = sem("piece_used")
        filled_a, emptied_a = sem("filled_a"), sem("emptied_a")
        filled_b, emptied_b = sem("filled_b"), sem("emptied_b")
        ones_set = sem("ones_set")
        cols_set = sem("cols_set")
        silu_done = sem("silu_done")
        mrow_ready = sem("mrow_ready")
        mod_ready = sem("mod_ready")
        lam_sums, lam_exps = sem("lam_sums"), sem("lam_exps")
        x_ready = [sem(f"x_ready{t}") for t in range(TILES)]
        root_ready = sem("root_ready")
        rs_ready = sem("rs_ready")
        xn_ready = sem("xn_ready")
        ss_ready, sq_ready = sem("ss_ready"), sem("sq_ready")
        tmp_ready = sem("tmp_ready")
        negmax_ready, exp_ready, mixed_ready = sem("negmax_ready"), sem("exp_ready"), sem("mixed_ready")
        o_ready = sem("o_ready")
        gd_ready = sem("gd_ready")
        top_ready, topexp_ready = sem("top_ready"), sem("topexp_ready")
        idx_ready = [sem(f"idx_ready{t}") for t in range(2)]
        landed = [sem(f"landed{j}") for j in range(RING)]
        fix_set, pool_step = sem("fix_set"), sem("pool_step")
        dots_ready, gelu_ready, wei_ready, diag_ready = (sem("dots_ready"), sem("gelu_ready"), sem("wei_ready"),
                                                          sem("diag_ready"))
        used_pe, used_dve = sem("used_pe"), sem("used_dve")
        vsum_read = sem("vsum_read")
        acc_zero = sem("acc_zero")
        y_ready, stored = sem("y_ready"), sem("stored")
        dve_step, act_step = sem("dve_step"), sem("act_step")

        block = ctx.enter_context(nc.Block())

        CONSTS = [(IDN[:, :], a["ident"]), (ROW[R_C:R_C + KD, :], a["c"].rearrange("b (k p) -> (b k) p", p=P)),
                  (ROW[R_CC:R_CC + KD, :], a["c_ctx"].rearrange("(k p) -> k p", p=P)),
                  (ROW[R_NA:R_NA + 16, :], a["norm_attn_g"].rearrange("l (k p) -> (l k) p", p=P)),
                  (ROW[R_NF:R_NF + 16, :], a["norm_ffn_g"].rearrange("l (k p) -> (l k) p", p=P)),
                  (ROW[R_QN:R_QN + 6, :], a["mla_q_norm_g"].rearrange("l (k p) -> (l k) p", p=P)),
                  (ROW[R_KN:R_KN + 4, :], a["mla_kv_norm_g"].rearrange("l (k p) -> (l k) p", p=P)),
                  (ROW[R_SN:R_SN + 2, :], a["diff_subnorm_g"]),
                  (BROW, a["b_ada"].rearrange("l (k p) -> (l k) p", p=P)),
                  (SK, a["peer_subkeys"].rearrange("l c k d -> k (l c) d")),
                  (SCR[:, 512:1024],
                   a["diff_lambda"].rearrange("l f d -> (l f d)").partition_broadcast(P)),
                  (ROPM[:, :, :, :], a["rope_mla"].rearrange("(t p) s n -> p t s n", p=P)),
                  (ROPD[:, :, :, :], a["rope_diff"].rearrange("(t p) s n -> p t s n", p=P)),
                  (IOTA[:, :], a["iota"].partition_broadcast(P))]
        CONSTS_ALL = 16 * len(CONSTS)

        def pieces(stage):
            kind, l = stage[0], (stage[1] if len(stage) > 1 else 0)
            if kind == "ada" and stage[2] < MODS // 4:
                w, (c0, n), ks = a["w_ada"][l], (stage[2] * W, W), (0, 4, 8)
            elif kind == "in":
                w, (c0, n), ks = a["w_in"][l], CHUNKS[stage[3]], (0, 4, 8)
            elif kind == "out":
                w, (c0, n), ks = a["w_out"][l], (stage[3] * W, W), (0, 4, 8)
            elif kind == "pick" and stage[3] < PH and stage[3] % 2 == 0:
                w, (c0, n), ks = a["peer_wq"][l], (stage[3] * 256, W), (0, 4, 8)
            elif kind == "up":
                ws = {"q": [("mla_wq_up", MH * MD, 3), ("mla_wq_rope", MH * RD, 3)], "k": [("mla_wk_up", MH * MD, 2)],
                      "v": [("mla_wv_up", MH * MD, 2)]}[stage[3]]
                return [(a[name][l].rearrange("(k p) n -> p k n", p=P), k, n) for name, n, k in ws]
            else:
                return []
            v = w.rearrange("(k p) n -> p k n", p=P)
            return [(v[:, ks[i]:ks[i + 1], c0:c0 + n], ks[i + 1] - ks[i], n) for i in range(2)]

        @block.sync
        def _(sp):
            for dst, src in CONSTS:
                sp.dma_start(dst, src).then_inc(consts_in, 16)
            xt = [a["ctx"][0, 0:P, :], a["ctx"][0, P:2 * P, :], a["x"][0, 0:P, :], a["x"][0, P:2 * P, :]]
            for t in range(TILES):
                sp.dma_start(X[:, t, :], xt[t]).then_inc(x_in, 16)
            n = 0
            for stage in PLAN:
                for src, k, cols in pieces(stage):
                    if n >= WSLOTS:
                        sp.wait_ge(piece_used, n - WSLOTS + 1)
                    sp.dma_start(WT[:, n % WSLOTS, 0:k, 0:cols], src).then_inc(piece_in[n % WSLOTS], 16)
                    n += 1
                if stage == ("close", 4):
                    sp.wait_ge(xn_ready, FINAL_GAIN_AFTER)
                    sp.dma_start(X[:, 0, :], a["final_norm_g"].partition_broadcast(P)).then_inc(fg_in, 16)
                if stage[0] == "last":
                    t = stage[1]
                    sp.wait_ge(y_ready, t + 1)
                    sp.dma_start(out[0, t * P:(t + 1) * P, :], X[:, 2 + t, :]).then_inc(stored, 16)
            sp.wait_ge(stored, 32)

        @block.gpsimd
        def _(pool):
            def unit(b, u, par, fixed):
                n = gu(b, u)

                def wait(s, v):
                    if not fixed:
                        pool.wait_ge(s, v)
                        pool.sem_inc(pool_step, 1)
                    elif v > 0:
                        pool.wait_ge(s, v)

                wait(used_pe, n * 4 - 3)
                at = bass.ds(u * UNIT, UNIT) if not fixed else slice(u * UNIT, (u + 1) * UNIT)
                pool.tensor_copy(FIX[:, par, :], IDX[:, b % HB, at]).then_inc(fix_set, 1)
                wait(fix_set, n + 1)
                for j in range(UNIT):
                    quad, i = j // 4, j % 4
                    if i < 2:
                        wait(used_pe, n * 4 + quad * 2 + i - 3)
                    else:
                        wait(used_dve, n * 4 + quad * 2 + i - 5)
                    pool.indirect_dma_start(
                        out=EXPERT[:, j, :], out_offset=None, in_=a["peer_uv"],
                        in_offset=bass.IndirectOffsetOnAxis(ap=FIX[:, par, j:j + 1], axis=0),
                    ).then_inc(landed[j], 16)

            for stage in PLAN:
                if stage[0] != "units":
                    continue
                _, b, u0, u1 = stage
                l, t = block_home(b)
                for kind, v0, v1 in parts_of(u0, u1):
                    pool.wait_ge(idx_ready[t % 2], 8 * (b // 2) + (v1 - 1) // 2 + 1)
                    if kind == "loop":
                        with pool.Fori(v0 // 2, v1 // 2) as pair:
                            for par in range(2):
                                unit(b, pair * 2 + par, par, False)
                    else:
                        unit(b, v0, v0 % 2, True)

        @block.tensor
        def _(pe):
            tick = Ticks()
            ra, rb = Ring(banks_a), Ring(banks_b)
            npiece = [0]

            def fill_a():
                bank, n = ra.next()
                if n > NA:
                    pe.wait_ge(emptied_a, n - NA)
                return bank

            def fill_b():
                bank, n = rb.next()
                if n > NB:
                    pe.wait_ge(emptied_b, n - NB)
                return bank

            def piece():
                n = npiece[0]
                npiece[0] += 1
                pe.wait_ge(piece_in[n % WSLOTS], 16 * (n // WSLOTS + 1))
                return WT[:, n % WSLOTS, :, :]

            def turn_tiles(bank, srcs, rows):
                for i, s in enumerate(srcs):
                    last = nc.tensor.transpose(bank[0:rows, i * P:(i + 1) * P], s, IDN[:, :])
                return last

            def consts(_):
                pe.wait_ge(consts_in, CONSTS_ALL)
                bank = fill_a()
                nc.tensor.transpose(bank[:, 0:ROWS], ROW, IDN[0:ROWS, 0:ROWS])
                nc.tensor.transpose(bank[:, P:P + 2 * MODS], BROW, IDN[0:2 * MODS, 0:2 * MODS]).then_inc(filled_a, 1)
                bank = fill_b()
                turn_tiles(bank, [SK[:, i, :] for i in range(4)], P).then_inc(filled_b, 1)

            def ada(stage):
                _, l, n = stage
                if n == 0:
                    pe.wait_ge(silu_done, 1)
                if n < MODS // 4:
                    bank = fill_b()
                    for half in range(2):
                        w = piece()
                        for k in range(4):
                            last = nc.tensor.matmul(bank[0:2, :], ST[:, :, 4 * half + k], w[:, k, :],
                                                    start=(half + k == 0), stop=(half == 1 and k == 3))
                            if half == 0 and k == 3:
                                last.then_inc(piece_used, 1)
                    last.then_inc(filled_b, 1)
                    pe.wait_ge(filled_b, rb.n)
                    pe.sem_inc(piece_used, 1)
                if n > 0:
                    pe.wait_ge(mrow_ready, l * (MODS // 4) + n)
                    bank = fill_a()
                    for k in range(4):
                        last = nc.tensor.transpose(bank[:, 2 * k:2 * k + 2], MROW[:, (n - 1) % 2, k * P:(k + 1) * P],
                                                   IDN[0:2, 0:2])
                    last.then_inc(filled_a, 1)

            def norm(stage):
                pe.wait_ge(xn_ready, tick("norm"))
                for half in range(2):
                    bank = fill_b()
                    turn_tiles(bank, [XN[:, (4 * half + k) * P:(4 * half + k + 1) * P] for k in range(4)], P)\
                        .then_inc(filled_b, 1)

            def norm2(stage):
                norm(stage)
                t = stage[3]
                pe.wait_ge(emptied_b, rb.n)
                for half in range(2):
                    bank = fill_a()
                    turn_tiles(bank, [HT[:, 4 * half + k, t * P:(t + 1) * P] for k in range(4)], P).then_inc(filled_a, 1)

            def product(stage):
                n = CHUNKS[stage[3]][1] if stage[0] == "in" else W
                pe.wait_ge(emptied_b, rb.n)
                two = [fill_a(), fill_a()]
                for half in range(2):
                    w = piece()
                    for t in range(2):
                        for k in range(4):
                            last = nc.tensor.matmul(two[t][:, 0:n], HT[:, 4 * half + k, t * P:(t + 1) * P], w[:, k, 0:n],
                                                    start=(half + k == 0), stop=(half == 1 and k == 3))
                        if half == 1:
                            last.then_inc(filled_a, 1)
                        elif t == 1:
                            last.then_inc(piece_used, 1)
                pe.wait_ge(filled_a, ra.n)
                pe.sem_inc(piece_used, 1)

            def gate_rows(n):
                pe.wait_ge(gd_ready, tick("gd"))
                bank = fill_a()
                for k in range(4):
                    last = nc.tensor.matmul(bank[:, k * P:(k + 1) * P], ONES[:, :], GD[:, k, :], start=True, stop=True)
                last.then_inc(filled_a, 1)

            def out_(stage):
                gate_rows(stage[3])
                product(stage)

            def up(stage):
                pe.wait_ge(emptied_b, rb.n)
                for k0, kn, n in {"q": [(0, 3, 512), (0, 3, 256)], "k": [(3, 2, 512)], "v": [(3, 2, 512)]}[stage[3]]:
                    w = piece()
                    for t in range(2):
                        bank = fill_a()
                        for k in range(kn):
                            last = nc.tensor.matmul(bank[:, 0:n], HT[:, k0 + k, t * P:(t + 1) * P], w[:, k, 0:n],
                                                    start=(k == 0), stop=(k == kn - 1))
                        last.then_inc(filled_a, 1)
                    pe.wait_ge(filled_a, ra.n)
                    pe.sem_inc(piece_used, 1)

            def turn(stage):
                what = stage[3]
                for t in range(2):
                    pe.wait_ge(tmp_ready, tick("tmp"))
                    if what in ("q", "k"):
                        src = ASM[:, (2 if what == "k" else 0) + t, :, :]
                        for half in range(2):
                            bank = fill_b()
                            turn_tiles(bank, [src[:, 4 * half + h, :] for h in range(4)], MQ).then_inc(filled_b, 1)
                    else:
                        src = TMP[:, tmp_slot(stage) + t, :]
                        cols = {"qd": 4, "kd": 4, "cq": 3, "kv": 2}[what]
                        bank = fill_b()
                        turn_tiles(bank, [src[:, k * P:(k + 1) * P] for k in range(cols)], P).then_inc(filled_b, 1)

            def attn(stage):
                _, l, g, t, i = stage
                keys = 2 * P if g == CTX else 4 * P
                if i == -1:
                    pe.wait_ge(emptied_b, rb.n)
                    pe.wait_ge(emptied_a, ra.n)
                if i + 1 < MH + DH:
                    h = i + 1
                    for c in range(1 if h < MH else 2):
                        bank = fill_b()
                        if h < MH:
                            q, k = QTM[:, h, t * P:(t + 1) * P], KTM[:, h, 0:keys]
                        else:
                            q = QTD[64 * c:64 * c + 64, h - MH, t * P:(t + 1) * P]
                            k = KTD[64 * c:64 * c + 64, h - MH, 0:keys]
                        nc.tensor.matmul(bank[:, 0:keys], q, k, start=True, stop=True).then_inc(filled_b, 1)
                if 0 <= i < MH + DH:
                    bank = fill_a()
                    if i < MH:
                        pe.wait_ge(exp_ready, tick.so_far("heads") + 1)
                    else:
                        pe.wait_ge(mixed_ready, tick("mixed"))
                    tick("heads")
                    turn_tiles(bank, [PR[:, i % 2, 0, k * P:(k + 1) * P] for k in range(keys // P)], P)\
                        .then_inc(filled_a, 1)
                    pt_fill.append(ra.n)
                if i >= 1:
                    h = i - 1
                    bank = fill_a()
                    pe.wait_ge(emptied_a, pt_fill.pop(0))
                    v = VM[:, :, h * MD:(h + 1) * MD] if h < MH else VD[:, :, (h - MH) * P:(h - MH + 1) * P]
                    n = MD if h < MH else P
                    for k in range(keys // P):
                        last = nc.tensor.matmul(bank[:, 0:n], PT[:, h % 2, k * P:(k + 1) * P], v[:, k, :],
                                                start=(k == 0), stop=(k == keys // P - 1))
                    last.then_inc(filled_a, 1)

            pt_fill = []

            def heads(stage):
                pe.wait_ge(o_ready, tick("o"))
                for half in range(2):
                    bank = fill_b()
                    turn_tiles(bank, [O[:, (4 * half + k) * P:(4 * half + k + 1) * P] for k in range(4)], P)\
                        .then_inc(filled_b, 1)

            held = {}

            def pick_(stage):
                _, l, g, h = stage
                if h == 0:
                    pe.wait_ge(emptied_b, rb.n)
                if h < PH:
                    if h % 2 == 0:
                        held["w"] = [piece(), piece()]
                    for c in range(2):
                        bank = fill_b()
                        for k in range(KD):
                            at = (h % 2) * 256 + c * P
                            last = nc.tensor.matmul(bank[:, 0:2 * P], held["w"][k // 4][:, k % 4, at:at + P], HT[:, k, :],
                                                    start=(k == 0), stop=(k == KD - 1))
                        last.then_inc(filled_b, 1)
                        held[h, c] = rb.n
                    if h % 2 == 1:
                        pe.wait_ge(filled_b, rb.n)
                        pe.sem_inc(piece_used, 2)
                if h >= 1:
                    pe.wait_ge(emptied_b, held[h - 1, 1])
                    for t in range(2):
                        bank = fill_a()
                        for c in range(2):
                            last = nc.tensor.matmul(bank[:, c * P:(c + 1) * P], QP[:, (h - 1) % 2, c, t * P:(t + 1) * P],
                                                    SKT[:, 2 * l + c, :], start=True, stop=True)
                        last.then_inc(filled_a, 1)

            def apply(q, par, first=False, last_one=False):
                for i in range(2):
                    pe.wait_ge(diag_ready, q * 2 + i + 1)
                    for n in range(2):
                        ins = nc.tensor.matmul(VSUM[n][:, :], DIAG[:, par, i, :],
                                               EXPERT[:, 4 * par + i, D + n * W:D + (n + 1) * W],
                                               start=(first and i == 0), stop=(last_one and i == 1))
                    ins.then_inc(used_pe, 1)

            def units(stage):
                _, b, u0, u1 = stage
                for kind, v0, v1 in parts_of(u0, u1):
                    if kind == "loop":
                        with pe.Fori(v0 // 2, v1 // 2) as pair:
                            for par in range(2):
                                q = pair * 4 + gu(b, par) * 2
                                apply(q - 1, 1)
                                apply(q, 0)
                    else:
                        q = 2 * gu(b, v0)
                        if v0 > 0:
                            apply(q - 1, 1)
                        else:
                            if b > 0:
                                pe.wait_ge(vsum_read, 2 * b)
                        apply(q, 0, first=(v0 == 0))

            def close(stage):
                b = stage[1]
                apply(2 * gu(b + 1, 0) - 1, 1, last_one=True)
                for n in range(2):
                    gate_rows(n)

            do = {"consts": consts, "ada": ada, "norm1": norm, "norm2": norm2, "in": product, "out": out_, "up": up,
                  "turn": turn, "attn": attn, "heads": heads, "pick": pick_, "units": units, "close": close}
            for stage in PLAN:
                if stage[0] in do:
                    do[stage[0]](stage)

        @block.scalar
        def _(act):
            tick = Ticks()
            rb = Ring(banks_b)
            steps = [0]

            def link(ins):
                steps[0] += 1
                ins.then_inc(act_step, 1)
                act.wait_ge(act_step, steps[0])

            def from_b():
                bank, n = rb.next()
                act.wait_ge(filled_b, n)
                return bank

            def consts(_):
                bank = from_b()
                nc.scalar.copy(SKT[:, :, :].rearrange("p i n -> p (i n)"), bank[:, :]).then_inc(emptied_b, 1)
                act.wait_ge(cols_set, 1)
                nc.scalar.activation(ST[:, :, :].rearrange("p c k -> p (c k)"), COL[:, 0, 0:2 * KD], ACT.Silu)\
                    .then_inc(silu_done, 1)
                act.wait_ge(lam_sums, 2 * DEPTH)
                nc.scalar.activation(LE[:, :], LS[:, :], ACT.Exp).then_inc(lam_exps, 1)

            def ada(stage):
                if stage[2] < MODS // 4:
                    bank = from_b()
                    nc.scalar.copy(MROW[:, stage[2] % 2, :], bank[0:2, :]).then_inc(emptied_b, 1)
                    act.wait_ge(emptied_b, rb.n)
                    act.sem_inc(mrow_ready, 1)

            def norm(stage):
                kind, l, g, t = stage
                tile = 2 * g + t
                if kind == "norm1" and l == 0:
                    act.wait_ge(x_in, 16 * TILES)
                else:
                    act.wait_ge(x_ready[tile], 2 * l + (kind == "norm2"))
                if kind == "norm1" and t == 0:
                    act.wait_ge(mod_ready, l + 1)
                link(nc.scalar.activation(XN, X[:, tile, :], ACT.Square, accum_out=NS[:, :]))
                nc.scalar.activation(NQ[:, :], NS[:, :], ACT.Sqrt, scale=1.0 / D, bias=EPST[:, :]).then_inc(root_ready, 1)
                act.wait_ge(rs_ready, tick("norm"))
                nc.scalar.activation(XN, X[:, tile, :], ACT.Copy, scale=NR[:, :]).then_inc(xn_ready, 1)
                at = (1 if kind == "norm1" else 4) * KD
                m = 1 - g
                for half in range(2):
                    bank = from_b()
                    for k in range(4):
                        j = at + 4 * half + k
                        last = nc.scalar.activation(HT[:, 4 * half + k, t * P:(t + 1) * P], bank[:, k * P:(k + 1) * P],
                                                    ACT.Identity, scale=MOD[:, l, j, m:m + 1],
                                                    bias=MOD[:, l, j - KD, m:m + 1])
                    last.then_inc(emptied_b, 1)

            def turn(stage):
                _, l, g, what = stage
                if what in ("cq", "kv"):
                    act.wait_ge(ss_ready, tick("ss"))
                    at = slice(0, 2) if what == "cq" else slice(2, 4)
                    nc.scalar.activation(SQ[:, at], SS[:, at], ACT.Sqrt, scale=1.0 / (QR if what == "cq" else KVR),
                                         bias=EPST[:, :]).then_inc(sq_ready, 1)
                for t in range(2):
                    keys = slice((2 * g + t) * P, (2 * g + t + 1) * P)
                    mine = slice(t * P, (t + 1) * P)
                    if what in ("q", "k"):
                        dst, at = (QTM, mine) if what == "q" else (KTM, keys)
                        for half in range(2):
                            bank = from_b()
                            nc.scalar.copy(dst[:, 4 * half:4 * half + 4, at],
                                           bank[0:MQ, :].rearrange("p (h n) -> p h n", h=4)).then_inc(emptied_b, 1)
                    elif what in ("qd", "kd"):
                        dst, at = (QTD, mine) if what == "qd" else (KTD, keys)
                        bank = from_b()
                        nc.scalar.copy(dst[:, :, at], bank[:, :].rearrange("p (h n) -> p h n", h=4))\
                            .then_inc(emptied_b, 1)
                    else:
                        k0, kn, r = (0, 3, R_QN + 3 * l) if what == "cq" else (3, 2, R_KN + 2 * l)
                        bank = from_b()
                        for k in range(kn):
                            last = nc.scalar.activation(HT[:, k0 + k, mine], bank[:, k * P:(k + 1) * P], ACT.Copy,
                                                        scale=COL[:, 0, r + k:r + k + 1])
                        last.then_inc(emptied_b, 1)

            def attn(stage):
                _, l, g, t, i = stage
                keys = 2 * P if g == CTX else 4 * P
                h = i + 1
                if h < MH + DH:
                    act.wait_ge(negmax_ready, tick("negmax"))
                    for c in range(1 if h < MH else 2):
                        bank = from_b()
                        ins = nc.scalar.activation(PR[:, h % 2, c, 0:keys], bank[:, 0:keys], ACT.Exp,
                                                   bias=NM[:, h % 2, c:c + 1], scale=SC_M if h < MH else SC_D,
                                                   accum_out=SUM[:, h % 2, c:c + 1])
                        ins.then_inc(emptied_b, 1)
                    act.wait_ge(emptied_b, rb.n)
                    act.sem_inc(exp_ready, 1)

            def heads(stage):
                _, l, g, t = stage
                act.wait_ge(ss_ready, tick("ss"))
                nc.scalar.activation(SQ[:, :], SS[:, :], ACT.Sqrt, scale=1.0 / P, bias=EPST[:, :]).then_inc(sq_ready, 1)
                for half in range(2):
                    bank = from_b()
                    src = bank[:, :].rearrange("p (h n) -> p h n", h=4)
                    dst = HT[:, 4 * half:4 * half + 4, t * P:(t + 1) * P]
                    if half == 0:
                        nc.scalar.copy(dst, src).then_inc(emptied_b, 1)
                    else:
                        nc.scalar.activation(dst, src, ACT.Copy, scale=SUBG[:, l:l + 1]).then_inc(emptied_b, 1)

            def pick_(stage):
                _, l, g, h = stage
                if h < PH:
                    for c in range(2):
                        bank = from_b()
                        nc.scalar.copy(QP[:, h % 2, c, :], bank[:, 0:2 * P]).then_inc(emptied_b, 1)
                if h >= 1:
                    for t in range(2):
                        act.wait_ge(top_ready, tick("top"))
                        nc.scalar.activation(TE[:, t, :], TS[:, t, :], ACT.Exp, bias=NT[:, t:t + 1],
                                             accum_out=TSUM[:, t:t + 1]).then_inc(topexp_ready, 1)

            def gelu(q, par):
                act.wait_ge(dots_ready, q + 1)
                nc.scalar.activation(GEL[:, par, :], DOT[:, par, :], ACT.Gelu).then_inc(gelu_ready, 1)

            def diag(q, par, fixed):
                act.wait_ge(wei_ready, q + 1)
                if not fixed or q >= 2:
                    act.wait_ge(used_pe, q * 2 - 2)
                for i in range(2):
                    nc.scalar.activation(DIAG[:, par, i, :], IDN[:, :], ACT.Copy, scale=WEI[:, par, i:i + 1])\
                        .then_inc(diag_ready, 1)

            def units(stage):
                _, b, u0, u1 = stage
                for kind, v0, v1 in parts_of(u0, u1):
                    if kind == "loop":
                        with act.Fori(v0 // 2, v1 // 2) as pair:
                            for par in range(2):
                                q = pair * 4 + gu(b, par) * 2
                                gelu(q, 0)
                                diag(q - 1, 1, False)
                                gelu(q + 1, 1)
                                diag(q, 0, False)
                    else:
                        q = 2 * gu(b, v0)
                        gelu(q, 0)
                        if v0 > 0:
                            diag(q - 1, 1, True)
                        gelu(q + 1, 1)
                        diag(q, 0, True)

            def close(stage):
                diag(2 * gu(stage[1] + 1, 0) - 1, 1, True)

            def last_(stage):
                t = stage[1]
                act.wait_ge(x_ready[2 + t], 4)
                link(nc.scalar.activation(XN, X[:, 2 + t, :], ACT.Square, accum_out=NS[:, :]))
                nc.scalar.activation(NQ[:, :], NS[:, :], ACT.Sqrt, scale=1.0 / D, bias=EPST[:, :]).then_inc(root_ready, 1)

            do = {"consts": consts, "ada": ada, "norm1": norm, "norm2": norm, "turn": turn, "attn": attn, "heads": heads,
                  "pick": pick_, "units": units, "close": close, "last": last_}
            for stage in PLAN:
                if stage[0] in do:
                    do[stage[0]](stage)

        @block.vector
        def _(dve):
            tick = Ticks()
            ra, rb = Ring(banks_a), Ring(banks_b)
            steps = [0]

            def link(ins):
                steps[0] += 1
                ins.then_inc(dve_step, 1)
                dve.wait_ge(dve_step, steps[0])

            def from_a():
                bank, n = ra.next()
                dve.wait_ge(filled_a, n)
                return bank

            def tt(o, x, y, op):
                return nc.vector.tensor_tensor(o, x, y, op)

            def consts(_):
                nc.vector.memset(EPST[:, :], EPS)
                nc.vector.memset(ONES[:, :], 1.0)
                dve.wait_ge(consts_in, CONSTS_ALL)
                bank = from_a()
                nc.vector.tensor_copy(COL[:, 0, 0:ROWS], bank[:, 0:ROWS]).then_inc(cols_set, 1)
                dve.wait_ge(cols_set, 1)
                link(nc.vector.tensor_copy(COL[:, 1, :], bank[:, P:P + 2 * MODS]))
                nc.vector.tensor_scalar(SUBG[:, 0:1], COL[:, 0, R_SN:R_SN + 1], 1.0 - lam_init(0), None, ALU.mult)
                nc.vector.tensor_scalar(SUBG[:, 1:2], COL[:, 0, R_SN + 1:R_SN + 2], 1.0 - lam_init(1), None, ALU.mult)\
                    .then_inc(emptied_a, 1)
                rb.next()
                for l in range(DEPTH):
                    for i in range(2):
                        nc.vector.tensor_tensor_reduce(out=LT[:, 2 * l + i, :], in0=LM[:, l, 2 * i, :], in1=LM[:, l, 2 * i + 1, :],
                                                       scale=1.0, scalar=0.0, op0=ALU.mult, op1=ALU.add,
                                                       accum_out=LS[:, 2 * l + i:2 * l + i + 1]).then_inc(lam_sums, 1)
                dve.wait_ge(lam_exps, 1)
                for l in range(DEPTH):
                    link(tt(LAM[:, l:l + 1], LE[:, 2 * l:2 * l + 1], LE[:, 2 * l + 1:2 * l + 2], ALU.subtract))
                    link(nc.vector.tensor_scalar(LAM[:, l:l + 1], LAM[:, l:l + 1], lam_init(l), None, ALU.add))

            def ada(stage):
                _, l, n = stage
                if n < MODS // 4:
                    rb.next()
                if n == 0:
                    return
                n -= 1
                bank = from_a()
                tt(MOD[:, l, 4 * n:4 * n + 4, :], bank[:, 0:8].rearrange("p (k c) -> p k c", c=2),
                   COL[:, 1, l * MODS + 4 * n:l * MODS + 4 * n + 4].unsqueeze(2).to_broadcast([P, 4, 2]),
                   ALU.add).then_inc(emptied_a, 1)

            def mod(stage):
                l = stage[1]
                dve.wait_ge(emptied_a, ra.n)
                for at, r in ((KD, R_NA), (4 * KD, R_NF)):
                    m = MOD[:, l, at:at + KD, :]
                    link(nc.vector.tensor_scalar(m, m, 1.0, None, ALU.add))
                    ins = tt(m, m, COL[:, 0, r + l * KD:r + (l + 1) * KD].unsqueeze(2).to_broadcast([P, KD, 2]), ALU.mult)
                    if at == KD:
                        link(ins)
                ins.then_inc(mod_ready, 1)
                dve.wait_ge(mod_ready, l + 1)

            def norm(stage):
                dve.wait_ge(root_ready, tick("norm"))
                nc.vector.reciprocal(NR[:, :], NQ[:, :]).then_inc(rs_ready, 1)
                rb.next()
                rb.next()

            def norm2(stage):
                norm(stage)
                _, l, g, t = stage
                b = blocks_of(l, g)[t]
                for half in range(2):
                    bank = from_a()
                    nc.vector.tensor_copy(H2[:, b % HB, half * W:(half + 1) * W], bank[:, :]).then_inc(emptied_a, 1)

            def rotate(dst, src, table, heads, width):
                def table_at(s, odd):
                    v = table[:, s, :].rearrange("p (n two) -> p n two", two=2)[:, :, odd]
                    return v.unsqueeze(1).to_broadcast([P, heads, width // 2])

                r = ROT[:, 0:heads * width].rearrange("p (h n) -> p h n", h=heads)
                r2 = r.rearrange("p h (n two) -> p h n two", two=2)
                s2 = src.rearrange("p h (n two) -> p h n two", two=2)
                tt(r2[:, :, :, 0], s2[:, :, :, 1], table_at(1, 0), ALU.mult)
                tt(r2[:, :, :, 1], s2[:, :, :, 0], table_at(1, 1), ALU.mult)
                link(tt(dst, src, table[:, 0, :].unsqueeze(1).to_broadcast([P, heads, width]), ALU.mult))
                return tt(dst, dst, r, ALU.add)

            def roots(at):
                dve.wait_ge(sq_ready, tick("sq"))
                link(nc.vector.reciprocal(RS[:, at], SQ[:, at]))

            def in_(stage):
                _, l, g, what = stage
                if what in pend_free and pend_free[what] in turned:
                    dve.wait_ge(filled_b, turned[pend_free[what]])
                for t in range(2):
                    bank = from_a()
                    tile = 2 * g + t
                    tmp = TMP[:, {"qd": 0, "kd": 2, "cq": 0, "kv": 2}.get(what, 0) + t, :]
                    if what == "vd":
                        nc.vector.tensor_copy(VD[:, tile, :], bank[:, :]).then_inc(emptied_a, 1)
                    elif what in ("qd", "kd"):
                        if g == LAT:
                            link(rotate(tmp.rearrange("p (h n) -> p h n", n=DD),
                                        bank[:, :].rearrange("p (h n) -> p h n", n=DD), ROPD[:, t, :, :], 2 * DH, DD))
                            free_a()
                            dve.sem_inc(tmp_ready, 1)
                        else:
                            link(nc.vector.tensor_copy(tmp, bank[:, :]))
                            free_a()
                            dve.sem_inc(tmp_ready, 1)
                    else:
                        n, c0 = (QR, 0) if what == "cq" else (KVR, 2)
                        link(nc.vector.tensor_copy(tmp[:, 0:n], bank[:, 0:n]))
                        if what == "kv":
                            kr = KR[:, t, :].unsqueeze(1)
                            src = bank[:, n:n + RD].unsqueeze(1)
                            if g == LAT:
                                link(rotate(kr, src, ROPM[:, t, :, :], 1, RD))
                            else:
                                link(nc.vector.tensor_copy(kr, src))
                        free_a()
                        ins = nc.vector.tensor_tensor_reduce(out=ROT[:, 0:n], in0=tmp[:, 0:n], in1=tmp[:, 0:n], scale=1.0,
                                                             scalar=0.0, op0=ALU.mult, op1=ALU.add,
                                                             accum_out=SS[:, c0 + t:c0 + t + 1])
                        if t == 0:
                            link(ins)
                        else:
                            ins.then_inc(ss_ready, 1)
                            dve.wait_ge(ss_ready, tick("ss"))

            def free_a():
                dve.sem_inc(emptied_a, 1)

            pend_free = {"cq": "qd", "kv": "kd"}
            turned = {}

            def turn(stage):
                _, l, g, what = stage
                if what in ("cq", "kv"):
                    n = QR if what == "cq" else KVR
                    c0 = 0 if what == "cq" else 2
                    roots(slice(c0, c0 + 2))
                    for t in range(2):
                        tmp = TMP[:, tmp_slot(stage) + t, 0:n]
                        nc.vector.tensor_scalar(tmp, tmp, RS[:, c0 + t:c0 + t + 1], None, ALU.mult).then_inc(tmp_ready, 1)
                for t in range(4 if what in ("q", "k") else 2):
                    rb.next()
                turned[what] = rb.n
                if what == "kv":
                    turned.clear()

            def up(stage):
                _, l, g, what = stage
                for t in range(2):
                    bank = from_a()
                    tile = 2 * g + t
                    if what == "v":
                        nc.vector.tensor_copy(VM[:, tile, :], bank[:, :]).then_inc(emptied_a, 1)
                        continue
                    asm = ASM[:, (2 if what == "k" else 0) + t, :, :]
                    nc.vector.tensor_copy(asm[:, :, 0:MD], bank[:, :].rearrange("p (h n) -> p h n", n=MD))\
                        .then_inc(emptied_a, 1)
                    if what == "k":
                        nc.vector.tensor_copy(asm[:, :, MD:MQ], KR[:, t, :].unsqueeze(1).to_broadcast([P, MH, RD]))\
                            .then_inc(tmp_ready, 1)
                if what == "q":
                    for t in range(2):
                        bank = from_a()
                        asm = ASM[:, t, :, :]
                        src = bank[:, 0:MH * RD].rearrange("p (h n) -> p h n", n=RD)
                        if g == LAT:
                            link(rotate(asm[:, :, MD:MQ], src, ROPM[:, t, :, :], MH, RD))
                        else:
                            link(nc.vector.tensor_copy(asm[:, :, MD:MQ], src))
                        free_a()
                        dve.sem_inc(tmp_ready, 1)

            def attn(stage):
                _, l, g, t, i = stage
                keys = 2 * P if g == CTX else 4 * P
                h = i + 1
                if h < MH + DH:
                    maps = 1 if h < MH else 2
                    for c in range(maps):
                        bank, n = rb.next()
                        dve.wait_ge(filled_b, n)
                        ins = nc.vector.reduce_max(MX[:, h % 2, c:c + 1], bank[:, 0:keys], AX_X)
                    link(ins)
                    nc.vector.tensor_scalar(NM[:, h % 2, 0:maps], MX[:, h % 2, 0:maps], -(SC_M if h < MH else SC_D), None,
                                            ALU.mult).then_inc(negmax_ready, 1)
                if 0 <= i < MH + DH:
                    maps = 1 if i < MH else 2
                    dve.wait_ge(exp_ready, tick("exp"))
                    link(nc.vector.reciprocal(INV[:, i % 2, 0:maps], SUM[:, i % 2, 0:maps]))
                    if i >= MH:
                        link(tt(INV[:, i % 2, 1:2], INV[:, i % 2, 1:2], LAM[:, l:l + 1], ALU.mult))
                        p0, p1 = PR[:, i % 2, 0, 0:keys], PR[:, i % 2, 1, 0:keys]
                        link(nc.vector.tensor_scalar(p1, p1, INV[:, i % 2, 1:2], None, ALU.mult))
                        nc.vector.scalar_tensor_tensor(out=p0, in0=p0, scalar=INV[:, i % 2, 0:1], in1=p1, op0=ALU.mult,
                                                       op1=ALU.subtract).then_inc(mixed_ready, 1)
                    bank = from_a()
                    nc.vector.tensor_copy(PT[:, i % 2, 0:keys], bank[:, 0:keys]).then_inc(emptied_a, 1)
                if i >= 1:
                    h = i - 1
                    bank = from_a()
                    if h < MH:
                        nc.vector.tensor_scalar(O[:, h * MD:(h + 1) * MD], bank[:, 0:MD], INV[:, h % 2, 0:1], None,
                                                ALU.mult).then_inc(emptied_a, 1)
                    else:
                        at = MH * MD + (h - MH) * P
                        nc.vector.tensor_copy(O[:, at:at + P], bank[:, 0:P]).then_inc(emptied_a, 1)

            def heads(stage):
                dve.wait_ge(emptied_a, ra.n)
                od = O[:, MH * MD:D].rearrange("p (h n) -> p h n", h=DH)
                sq = PT[:, 0, :].rearrange("p (h n) -> p h n", h=DH)
                link(tt(sq, od, od, ALU.mult))
                nc.vector.tensor_reduce(SS[:, :], sq, AX_X, ALU.add).then_inc(ss_ready, 1)
                tick("ss")
                roots(slice(0, 4))
                tt(od, od, RS[:, :].unsqueeze(2).to_broadcast([P, DH, P]), ALU.mult).then_inc(o_ready, 1)
                rb.next()
                rb.next()

            def diagonals(l, g, which, n):
                at = (2 if which == 1 else 5) * KD + 4 * n
                m = 1 - g
                tt(GD[:, :, :], IDN[:, :].unsqueeze(1).to_broadcast([P, 4, P]),
                   MOD[:, l, at:at + 4, m:m + 1].to_broadcast([P, 4, P]), ALU.mult).then_inc(gd_ready, 1)

            def out_(stage):
                _, l, g, n = stage
                diagonals(l, g, 1, n)
                bank = from_a()
                nc.vector.tensor_copy(GROW, bank[:, :]).then_inc(emptied_a, 1)
                dve.wait_ge(emptied_a, ra.n)
                for t in range(2):
                    bank = from_a()
                    x = X[:, 2 * g + t, n * W:(n + 1) * W]
                    tt(YT[:, t, :], bank[:, :], GROW, ALU.mult).then_inc(emptied_a, 1)
                    dve.wait_ge(emptied_a, ra.n)
                    ins = tt(x, x, YT[:, t, :], ALU.add)
                    if n == 1:
                        ins.then_inc(x_ready[2 * g + t], 1)

            def pick_(stage):
                _, l, g, h = stage
                if h < PH:
                    rb.next()
                    rb.next()
                if h == 0:
                    return
                h -= 1
                for t in range(2):
                    b = blocks_of(l, g)[t]
                    bank = from_a()
                    for c in range(2):
                        s = bank[:, c * P:(c + 1) * P]
                        link(nc.vector.max(SV[:, c, 0:8], s))
                        nc.vector.max_index(SI[:, c, 0:8], SV[:, c, 0:8], s)
                        link(nc.vector.match_replace(WK[:, c, :], SV[:, c, 0:8], s, LOWEST))
                        link(nc.vector.max(SV[:, c, 8:16], WK[:, c, :]))
                        link(nc.vector.max_index(SI[:, c, 8:16], SV[:, c, 8:16], WK[:, c, :]))
                    free_a()
                    nc.vector.tensor_copy(SIF[:, :, :], SI[:, :, :])
                    cand = CAND.rearrange("p (i j) -> p i j", i=TOPK)
                    link(tt(cand, SV[:, 0, :].unsqueeze(2).to_broadcast([P, TOPK, TOPK]),
                            SV[:, 1, :].unsqueeze(1).to_broadcast([P, TOPK, TOPK]), ALU.add))
                    link(nc.vector.max(TS[:, t, 0:8], CAND))
                    nc.vector.max_index(POS[:, 0:8], TS[:, t, 0:8], CAND)
                    link(nc.vector.match_replace(CANW, TS[:, t, 0:8], CAND, LOWEST))
                    link(nc.vector.max(TS[:, t, 8:16], CANW))
                    nc.vector.tensor_scalar(NT[:, t:t + 1], TS[:, t, 0:1], -1.0, None, ALU.mult).then_inc(top_ready, 1)
                    link(nc.vector.max_index(POS[:, 8:16], TS[:, t, 8:16], CANW))
                    nc.vector.tensor_scalar(AB[:, 0, :], POS[:, :], 4, None, ALU.logical_shift_right)
                    link(nc.vector.tensor_scalar(AB[:, 1, :], POS[:, :], 15, None, ALU.bitwise_and))
                    link(nc.vector.tensor_copy(ABF[:, :, :], AB[:, :, :]))
                    for c in range(2):
                        tt(HOT[:, c], ABF[:, c, :].unsqueeze(2).to_broadcast([P, TOPK, TOPK]),
                           IOTA[:, :].unsqueeze(1).to_broadcast([P, TOPK, TOPK]), ALU.is_equal).then_inc(dve_step, 1)
                        steps[0] += 1
                    dve.wait_ge(dve_step, steps[0])
                    for c in range(2):
                        ins = tt(HOT[:, c], HOT[:, c], SIF[:, c, :].unsqueeze(1).to_broadcast([P, TOPK, TOPK]), ALU.mult)
                    link(ins)
                    link(nc.vector.tensor_reduce(PICK[:, :, :], HOT, AX_X, ALU.add))
                    at = slice(h * TOPK, (h + 1) * TOPK)
                    link(nc.vector.scalar_tensor_tensor(out=PICK[:, 0, :], in0=PICK[:, 0, :], scalar=float(NK),
                                                        in1=PICK[:, 1, :], op0=ALU.mult, op1=ALU.add))
                    link(nc.vector.tensor_scalar(IDX[:, b % HB, at], PICK[:, 0, :], float(l * NK * NK), None, ALU.add))
                    dve.wait_ge(topexp_ready, tick("topexp"))
                    link(nc.vector.reciprocal(TINV[:, t:t + 1], TSUM[:, t:t + 1]))
                    nc.vector.tensor_scalar(GATE[:, b % HB, at], TE[:, t, :], TINV[:, t:t + 1], None, ALU.mult)\
                        .then_inc(idx_ready[t], 1)
                    dve.wait_ge(idx_ready[t], 8 * (b // 2) + h + 1)

            def dots(b, n, par):
                for i in range(4):
                    j = 4 * par + i
                    dve.wait_ge(landed[j], (n + 1) * 16)
                    ins = nc.vector.tensor_tensor_reduce(out=EXPERT[:, j, 0:D], in0=EXPERT[:, j, 0:D], in1=H2[:, b % HB, :],
                                                         scale=1.0, scalar=0.0, op0=ALU.mult, op1=ALU.add,
                                                         accum_out=DOT[:, par, i:i + 1])
                ins.then_inc(dots_ready, 1)

            def apply(b, u, q, par, fixed):
                dve.wait_ge(gelu_ready, q + 1)
                if not fixed or q >= 2:
                    dve.wait_ge(diag_ready, q * 2 - 2)
                at = bass.ds(u * UNIT + 4 * par, 4) if not fixed else slice(u * UNIT + 4 * par, u * UNIT + 4 * par + 4)
                tt(WEI[:, par, :], GEL[:, par, :], GATE[:, b % HB, at], ALU.mult).then_inc(wei_ready, 1)
                dve.wait_ge(wei_ready, q + 1)
                for i in range(2):
                    if not fixed or q + i > 0:
                        dve.wait_ge(used_dve, q * 2 + i)
                    nc.vector.scalar_tensor_tensor(out=ACC[:, :], in0=EXPERT[:, 4 * par + 2 + i, D:2 * D],
                                                   scalar=WEI[:, par, 2 + i:3 + i], in1=ACC[:, :], op0=ALU.mult,
                                                   op1=ALU.add).then_inc(used_dve, 1)

            def units(stage):
                _, b, u0, u1 = stage
                for kind, v0, v1 in parts_of(u0, u1):
                    if kind == "loop":
                        with dve.Fori(v0 // 2, v1 // 2) as pair:
                            for par in range(2):
                                n = pair * 2 + gu(b, par)
                                dots(b, n, 0)
                                apply(b, pair * 2 + (par - 1), n * 2 - 1, 1, False)
                                dots(b, n, 1)
                                apply(b, pair * 2 + par, n * 2, 0, False)
                    else:
                        n = gu(b, v0)
                        if v0 == 0:
                            nc.vector.memset(ACC[:, :], 0.0).then_inc(acc_zero, 1)
                            dve.wait_ge(acc_zero, b + 1)
                        dots(b, n, 0)
                        if v0 > 0:
                            apply(b, v0 - 1, 2 * n - 1, 1, True)
                        dots(b, n, 1)
                        apply(b, v0, 2 * n, 0, True)

            def close(stage):
                b = stage[1]
                l, tile = block_home(b)
                q = 2 * gu(b + 1, 0) - 1
                apply(b, UNITS - 1, q, 1, True)
                dve.wait_ge(used_dve, 2 * q + 2)
                dve.wait_ge(used_pe, 2 * q + 2)
                for n in range(2):
                    half = slice(n * W, (n + 1) * W)
                    diagonals(l, tile // 2, 2, n)
                    tt(ACC[:, half], ACC[:, half], VSUM[n][:, :], ALU.add).then_inc(vsum_read, 1)
                    rows = from_a()
                    dve.wait_ge(vsum_read, 2 * b + n + 1)
                    link(tt(ACC[:, half], ACC[:, half], rows[:, :], ALU.mult))
                    free_a()
                    x = X[:, tile, half]
                    ins = tt(x, x, ACC[:, half], ALU.add)
                    if n == 1:
                        ins.then_inc(x_ready[tile], 1)
                        dve.wait_ge(x_ready[tile], 2 * l + 2)

            def last_(stage):
                t = stage[1]
                dve.wait_ge(root_ready, tick("norm"))
                nc.vector.reciprocal(NR[:, :], NQ[:, :]).then_inc(rs_ready, 1)
                dve.wait_ge(rs_ready, tick.so_far("norm"))
                dve.wait_ge(fg_in, 16)
                x = X[:, 2 + t, :]
                nc.vector.scalar_tensor_tensor(out=x, in0=x, scalar=NR[:, :], in1=X[:, 0, :], op0=ALU.mult,
                                               op1=ALU.mult).then_inc(y_ready, 1)

            do = {"consts": consts, "ada": ada, "mod": mod, "norm1": norm, "norm2": norm2, "in": in_, "out": out_,
                  "up": up, "turn": turn, "attn": attn, "heads": heads, "pick": pick_, "units": units, "close": close,
                  "last": last_}
            for stage in PLAN:
                if stage[0] in do:
                    do[stage[0]](stage)


_INS = ["x", "c", "ctx", "c_ctx", "norm_attn_g", "norm_ffn_g", "w_ada", "b_ada", "w_in", "mla_q_norm_g", "mla_wq_up",
        "mla_wq_rope", "mla_kv_norm_g", "mla_wk_up", "mla_wv_up", "diff_lambda", "diff_subnorm_g", "w_out", "peer_wq",
        "peer_subkeys", "final_norm_g"]


def rope_table(np, width, seq=256, grid=64, base=10000.0):
    quarter = width // 4
    freq = (np.float32(base) ** (-np.arange(quarter, dtype=np.float32) / np.float32(quarter))).astype(np.float32)
    row = np.repeat(np.arange(seq // grid, dtype=np.float32), grid)
    col = np.tile(np.arange(grid, dtype=np.float32), seq // grid)
    ang = np.concatenate([row[:, None] * freq, col[:, None] * freq], axis=-1)
    cos = np.repeat(np.cos(ang), 2, axis=-1)
    sin = np.repeat(np.sin(ang), 2, axis=-1) * np.tile(np.array([-1.0, 1.0], np.float32), width // 2)
    return np.stack([cos, sin], axis=1).astype(np.float32)


def kernel(**inputs):
    import numpy as np
    import concourse.bacc as bacc
    from concourse.bass_utils import run_bass_kernel_spmd

    nc = bacc.Bacc("TRN2", target_bir_lowering=False, num_devices=1)
    host = {n: np.asarray(inputs[n]) for n in _INS}
    u, v = np.asarray(inputs["peer_u"]), np.asarray(inputs["peer_v"])
    host["peer_uv"] = np.concatenate([u, v], axis=-1).reshape(-1, u.shape[-1] + v.shape[-1])
    host["ident"] = np.eye(P, dtype=np.float32)
    host["iota"] = np.arange(TOPK, dtype=np.float32)
    host["rope_mla"] = rope_table(np, RD)
    host["rope_diff"] = rope_table(np, DD)
    arrays, aps = {}, {}
    for name, arr in host.items():
        arr = np.ascontiguousarray(arr)
        arrays[f"in_{name}"] = arr
        aps[name] = nc.dram_tensor(f"in_{name}", arr.shape, mybir.dt.from_np(arr.dtype), kind="ExternalInput").ap()
    out = nc.dram_tensor("out_y", (1, 256, D), F32, kind="ExternalOutput").ap()
    backbone(nc, aps, out)
    got = run_bass_kernel_spmd(nc, [arrays], core_ids=[0])
    return got.results[0]["out_y"]
```

```python
import math
from contextlib import ExitStack

import concourse.bass as bass
from concourse import mybir

F32 = mybir.dt.float32
U32 = mybir.dt.uint32
ALU = mybir.AluOpType
ACT = mybir.ActivationFunctionType
AX_X = mybir.AxisListType.X

P = 128
D = 1024
KD = D // P
DEPTH = 2
TILES = 4
EPS = 1e-6
QR, KVR, RD = 384, 256, 32
MH, MD = 8, 64
MQ = MD + RD
DH, DD = 4, 64
PH, TOPK, NK = 8, 16, 128
SLOTS = PH * TOPK
W = 512
NA = 3
NB = 3
WSLOTS = 2
RING = 8
HB = 3
UNIT = 8
QUADS = SLOTS // 4
BOTH = (0, 1)
CTX, LAT = 0, 1
CHUNKS = {"cq": (0, 384), "kv": (384, 288), "qd": (672, 512), "kd": (1184, 512), "vd": (1696, 512)}
SC_M = MQ ** -0.5
SC_D = DD ** -0.5
LOWEST = -3.0e38

R_C, R_CC, R_NA, R_NF, R_QN, R_KN, R_SN = 0, 8, 16, 32, 48, 54, 58
ROWS = 60
MODS = 6 * KD


def lam_init(l):
    return 0.8 - 0.6 * math.exp(-0.3 * l)


def blocks_of(l, g):
    return [4 * l + 2 * g - (2 if l else 0) + t for t in range(2)]


def block_home(b):
    return (0, b) if b < 4 else (1, b - 2)


def front(l, g, ts=BOTH):
    full = not (l == DEPTH - 1 and g == CTX)
    out = [("stat", l, g, t, 1) for t in ts] + [("norm", l, g, t, 1) for t in ts]
    names = (["qd"] if full else []) + ["kd", "vd"] + (["cq"] if full else []) + ["kv"]
    prior = None
    for n in names:
        out += [("in", l, g, n, ts, half) for half in range(2)]
        if prior and prior != "vd":
            out.append(("turn", l, g, prior, ts))
        if n in ("cq", "kv"):
            out.append(("root", l, g, n, ts))
        prior = n
    out.append(("turn", l, g, "kv", ts))
    if full:
        out += [("up", l, g, "q", ts), ("up", l, g, "r", ts), ("up", l, g, "k", ts), ("turn", l, g, "q", ts),
                ("up", l, g, "v", ts), ("turn", l, g, "k", ts)]
    else:
        out += [("up", l, g, "k", ts), ("up", l, g, "v", ts), ("turn", l, g, "k", ts)]
    return out


def attention(l, g):
    out = []
    for t in BOTH:
        out += [("attn", l, g, t, i) for i in range(-1, MH + DH + 1)]
        out += [("hnorm", l, g, t), ("heads", l, g, t)]
    return out


def outward(l, g):
    out = []
    for n in range(2):
        out += [("gates", l, g, n)] + [("out", l, g, n, BOTH, half) for half in range(2)]
    out += [("stat", l, g, t, 2) for t in BOTH]
    for t in BOTH:
        out += [("norm", l, g, t, 2), ("back", l, g, t)]
    return out


def pick(l, g):
    return [("pick", l, g, h) for h in range(PH + 1)]


def modulation(l, n0, n1):
    out = []
    for n in range(n0, n1):
        out.append(("ada", l, n))
        if n > n0:
            out.append(("adat", l, n - 1))
    return out + [("adat", l, n1 - 1)]


COST = {"stat": 3, "norm": 4, "in": 7, "turn": 2, "root": 1, "up": 5, "attn": 3, "hnorm": 2, "heads": 3, "gates": 1, "out": 8,
        "back": 2, "pick": 14, "ada": 7, "adat": 1, "mod": 1}


def weave(background, stream):
    out, at, done = [], 0, 0
    total = sum(COST[s[0]] for s in background)
    for n, s in enumerate(background):
        out.append(s)
        done += COST[s[0]]
        to = len(stream) if n == len(background) - 1 else done * len(stream) // total
        while at < to and not (stream[at][0] == "close" and s[0] in ("in", "out") and s[-1] == 0):
            out.append(stream[at])
            at += 1
    return out


def spans(plan):
    out = []
    for s in plan:
        if s[0] == "quads" and out and out[-1][0] == "quads" and out[-1][1] == s[1] and out[-1][3] == s[2]:
            out[-1] = ("quads", s[1], out[-1][2], s[3])
        else:
            out.append(s)
    return out


def stream_of(b, first=0, last=QUADS):
    return [("quads", b, q, q + 1) for q in range(first, last)] + ([("close", b)] if last == QUADS else [])


EARLY = 24


def first_picks(l, g):
    picks, b = pick(l, g), blocks_of(l, g)[0]
    out = picks[0:2]
    for n, s in enumerate(picks[2:]):
        out += [s] + stream_of(b, EARLY * n // 7, EARLY * (n + 1) // 7)
    return out


def make_plan():
    plan = [("consts",)]
    plan += modulation(0, 0, 4) + [("mod", 0, 1)] + front(0, CTX)
    rest, attn = modulation(0, 4, 12), attention(0, CTX)
    for n, s in enumerate(attn):
        plan.append(s)
        plan += rest[n * len(rest) // len(attn):(n + 1) * len(rest) // len(attn)]
    plan += [("mod", 0, 2)] + outward(0, CTX) + first_picks(0, CTX)
    plan += weave(front(0, LAT) + attention(0, LAT) + outward(0, LAT) + pick(0, LAT), stream_of(0, EARLY) + stream_of(1))
    plan += weave(modulation(1, 0, 12) + [("mod", 1, 1), ("mod", 1, 2)] + front(1, CTX), stream_of(2))
    plan += weave(front(1, LAT, (0,)), stream_of(3))
    plan += front(1, LAT, (1,)) + attention(1, LAT) + outward(1, LAT) + first_picks(1, LAT)
    plan += [("picked",)] + stream_of(4, EARLY) + [("last", 0)] + stream_of(5) + [("last", 1)]
    at = {s: n for n, s in enumerate(plan)}
    for b in range(HB, 6):
        l, tile = block_home(b)
        assert at["close", b - HB] < at["back", l, tile // 2, tile % 2], "the inputs of block b - 3 are still in use"
    return spans(plan)


PLAN = make_plan()


def late(plan):
    out = []
    for s in plan:
        if s[0] == "quads" and out and out[-1][0] not in ("quads", "close", "last"):
            out.insert(len(out) - 1, s)
        else:
            out.append(s)
    at = {s: n for n, s in enumerate(out)}
    for s in out:
        if s[0] == "quads":
            l, tile = block_home(s[1])
            assert at["pick", l, tile // 2, (s[3] - 1) // 4 + 1] < at[s], "quads before their pick"
    return out


FINAL_GAIN_AFTER = sum(s[0] == "norm" for s in PLAN)


def parts_of(q0, q1):
    out, q = [], q0
    while q < q1:
        m = (q1 - q) // 4 * 4
        if q1 == QUADS:
            m = (q1 - 1 - q) // 4 * 4
        if q % 4 == 0 and q > 0 and m >= 8:
            out.append(("loop", q, q + m))
            q += m
        else:
            out.append(("one", q, q + 1))
            q += 1
    return out


def tmp_slot(name):
    return {"qd": 0, "kd": 2, "cq": 0, "kv": 2}[name]


def root_at(name, t):
    return (0 if name == "cq" else 2) + t


def slot_no(b, q, i=0):
    return b * SLOTS + q * 4 + i


class Ring:

    def __init__(self, banks):
        self.banks, self.n = banks, 0

    def next(self):
        self.n += 1
        return self.banks[(self.n - 1) % len(self.banks)], self.n


class Ticks:

    def __init__(self):
        self.n = {}

    def __call__(self, name):
        self.n[name] = self.n.get(name, 0) + 1
        return self.n[name]

    def so_far(self, name):
        return self.n.get(name, 0)


def backbone(nc, a, out):
    ctx = ExitStack()
    with ctx:
        def sb(name, shape, dt=F32):
            return ctx.enter_context(nc.sbuf_tensor(name, shape, dt))

        def sem(name):
            return ctx.enter_context(nc.semaphore(name))

        X = sb("X", [P, TILES, D])
        H2 = sb("H2", [P, HB, D])
        HT = sb("HT", [P, KD, 2 * P])
        KTM = sb("KTM", [MQ, MH, TILES * P])
        VM = sb("VM", [P, TILES, MH * MD])
        KTD = sb("KTD", [P, DH, TILES * P])
        VD = sb("VD", [P, TILES, DH * 2 * DD])
        QTM = sb("QTM", [MQ, MH, 2 * P])
        QTD = sb("QTD", [P, DH, 2 * P])
        EXPERT = sb("EXPERT", [P, RING, 2 * D])
        WT = sb("WT", [P, WSLOTS, 4, W])
        SCR = sb("SCR", [P, 4096])
        ACC = sb("ACC", [P, D])
        IDX = sb("IDX", [P, HB, SLOTS], U32)
        GATE = sb("GATE", [P, HB, SLOTS])
        FIX = sb("FIX", [P, 2, UNIT], U32)
        IDN = sb("IDN", [P, P])
        ONES = sb("ONES", [P, P])
        GD = sb("GD", [P, 4, P])
        DIAG = sb("DIAG", [P, 2, P])
        COL = sb("COL", [P, 2, 2 * MODS])
        ST = sb("ST", [P, 2, KD])
        MROW = sb("MROW", [2, 2, W])
        MOD = sb("MOD", [P, DEPTH, MODS, 2])
        SKT = sb("SKT", [P, DEPTH * 2, P])
        LS = sb("LS", [P, 2 * DEPTH])
        LE = sb("LE", [P, 2 * DEPTH])
        LAM = sb("LAM", [P, DEPTH])
        SUBG = sb("SUBG", [P, DEPTH])
        ROPM = sb("ROPM", [P, 2, 2, RD])
        ROPD = sb("ROPD", [P, 2, 2, DD])
        IOTA = sb("IOTA", [P, TOPK])
        EPST = sb("EPST", [P, 1])
        KR = sb("KR", [P, 2, RD])
        SS = sb("SS", [P, 4])
        SQ = sb("SQ", [P, 4])
        RS = sb("RS", [P, 4])
        NS = sb("NS", [P, 1])
        NQ = sb("NQ", [P, 1])
        NR = sb("NR", [P, 1])
        MX = sb("MX", [P, 2, 2])
        NM = sb("NM", [P, 2, 2])
        SUM = sb("SUM", [P, 2, 2])
        INV = sb("INV", [P, 2, 2])
        SV = sb("SV", [P, 2, TOPK])
        SI = sb("SI", [P, 2, TOPK], U32)
        SIF = sb("SIF", [P, 2, TOPK])
        TS = sb("TS", [P, 2, TOPK])
        POS = sb("POS", [P, TOPK], U32)
        AB = sb("AB", [P, 2, TOPK], U32)
        ABF = sb("ABF", [P, 2, TOPK])
        PICK = sb("PICK", [P, 2, TOPK])
        TE = sb("TE", [P, 2, TOPK])
        NT = sb("NT", [P, 2])
        TSUM = sb("TSUM", [P, 2])
        TINV = sb("TINV", [P, 2])
        DOT = sb("DOT", [P, 4])
        GEL = sb("GEL", [P, 4])
        WEI = sb("WEI", [P, 4])

        SK = SCR[:, 0:DEPTH * 2 * P].rearrange("p (i n) -> p i n", n=P)
        LM = SCR[:, 512:1024].rearrange("p (l f n) -> p l f n", l=DEPTH, f=4)
        ROW = SCR[0:ROWS, 1024:1024 + P]
        BROW = SCR[0:2 * MODS, 1536:1536 + P]
        LT = SCR[:, 2048:2048 + 2 * DEPTH * DD].rearrange("p (i n) -> p i n", n=DD)
        XN = SCR[:, 0:2 * D].rearrange("p (t n) -> p t n", t=2)
        ROT = SCR[:, 0:W]
        TMP = SCR[:, D:D + 4 * W].rearrange("p (s n) -> p s n", s=4)
        ASM = SCR[:, D:4096].rearrange("p (s h n) -> p s h n", s=4, h=MH)
        PR = SCR[:, 0:2048].rearrange("p (r c n) -> p r c n", r=2, c=2)
        PT = SCR[:, 2048:3072].rearrange("p (r n) -> p r n", r=2)
        O = SCR[:, 3072:4096]
        YT = SCR[:, D:D + 2 * W].rearrange("p (s n) -> p s n", s=2)
        GROW = SCR[:, D + 2 * W:D + 3 * W]
        WK = SCR[:, D:D + 256].rearrange("p (c n) -> p c n", c=2)
        CAND = SCR[:, D + 256:D + 512]
        CANW = SCR[:, D + 512:D + 768]
        HOT = SCR[:, D + 1024:D + 1536].rearrange("p (c s n) -> p c s n", c=2, s=TOPK)
        QP = SCR[:, 3072:4096].rearrange("p (r c n) -> p r c n", r=2, c=2)

        banks_a = [ctx.enter_context(nc.psum_tensor(f"PA{i}", [P, W], F32)) for i in range(NA)]
        banks_b = [ctx.enter_context(nc.psum_tensor(f"PB{i}", [P, W], F32)) for i in range(NB)]
        VSUM = [ctx.enter_context(nc.psum_tensor(f"VS{i}", [P, W], F32)) for i in range(2)]

        consts_in = sem("consts_in")
        x_in = sem("x_in")
        fg_in = sem("fg_in")
        piece_in = [sem(f"piece_in{i}") for i in range(WSLOTS)]
        piece_used = sem("piece_used")
        filled_a, emptied_a = sem("filled_a"), sem("emptied_a")
        filled_b, emptied_b = sem("filled_b"), sem("emptied_b")
        ones_set = sem("ones_set")
        cols_set = sem("cols_set")
        silu_done = sem("silu_done")
        mrow_ready = sem("mrow_ready")
        mod_ready = sem("mod_ready")
        lam_sums, lam_exps = sem("lam_sums"), sem("lam_exps")
        x_ready = [sem(f"x_ready{t}") for t in range(TILES)]
        root_ready = sem("root_ready")
        rs_ready = sem("rs_ready")
        xn_ready = sem("xn_ready")
        ss_ready, sq_ready = sem("ss_ready"), sem("sq_ready")
        tmp_ready = sem("tmp_ready")
        negmax_ready, exp_ready, mixed_ready = sem("negmax_ready"), sem("exp_ready"), sem("mixed_ready")
        o_ready = sem("o_ready")
        gd_ready = sem("gd_ready")
        top_ready, topexp_ready = sem("top_ready"), sem("topexp_ready")
        idx_ready = [sem(f"idx_ready{t}") for t in range(2)]
        landed = [sem(f"landed{j}") for j in range(RING)]
        fix_set, pool_step = sem("fix_set"), sem("pool_step")
        dots_ready, gelu_ready, wei_ready, diag_ready = (sem("dots_ready"), sem("gelu_ready"), sem("wei_ready"),
                                                          sem("diag_ready"))
        used_pe, used_dve = sem("used_pe"), sem("used_dve")
        vsum_read = sem("vsum_read")
        acc_zero = sem("acc_zero")
        y_ready, stored = sem("y_ready"), sem("stored")
        dve_step, act_step = sem("dve_step"), sem("act_step")

        block = ctx.enter_context(nc.Block())

        CONSTS = [(IDN[:, :], a["ident"]), (ROW[R_C:R_C + KD, :], a["c"].rearrange("b (k p) -> (b k) p", p=P)),
                  (ROW[R_CC:R_CC + KD, :], a["c_ctx"].rearrange("(k p) -> k p", p=P)),
                  (ROW[R_NA:R_NA + 16, :], a["norm_attn_g"].rearrange("l (k p) -> (l k) p", p=P)),
                  (ROW[R_NF:R_NF + 16, :], a["norm_ffn_g"].rearrange("l (k p) -> (l k) p", p=P)),
                  (ROW[R_QN:R_QN + 6, :], a["mla_q_norm_g"].rearrange("l (k p) -> (l k) p", p=P)),
                  (ROW[R_KN:R_KN + 4, :], a["mla_kv_norm_g"].rearrange("l (k p) -> (l k) p", p=P)),
                  (ROW[R_SN:R_SN + 2, :], a["diff_subnorm_g"]),
                  (BROW, a["b_ada"].rearrange("l (k p) -> (l k) p", p=P)),
                  (SK, a["peer_subkeys"].rearrange("l c k d -> k (l c) d")),
                  (SCR[:, 512:1024],
                   a["diff_lambda"].rearrange("l f d -> (l f d)").partition_broadcast(P)),
                  (ROPM[:, :, :, :], a["rope_mla"].rearrange("(t p) s n -> p t s n", p=P)),
                  (ROPD[:, :, :, :], a["rope_diff"].rearrange("(t p) s n -> p t s n", p=P)),
                  (IOTA[:, :], a["iota"].partition_broadcast(P))]
        CONSTS_ALL = 16 * len(CONSTS)

        def pieces(stage):
            kind, l = stage[0], (stage[1] if len(stage) > 1 else 0)
            if kind == "ada":
                w, (c0, n), ks = a["w_ada"][l], (stage[2] * W, W), (0, 4, 8)
            elif kind == "in" and stage[5] == 0:
                w, (c0, n), ks = a["w_in"][l], CHUNKS[stage[3]], (0, 4, 8)
            elif kind == "out" and stage[5] == 0:
                w, (c0, n), ks = a["w_out"][l], (stage[3] * W, W), (0, 4, 8)
            elif kind == "pick" and stage[3] < PH and stage[3] % 2 == 0:
                w, (c0, n), ks = a["peer_wq"][l], (stage[3] * 256, W), (0, 4, 8)
            elif kind == "up":
                ws = {"q": [("mla_wq_up", MH * MD, 3)], "r": [("mla_wq_rope", MH * RD, 3)], "k": [("mla_wk_up", MH * MD, 2)],
                      "v": [("mla_wv_up", MH * MD, 2)]}[stage[3]]
                return [(a[name][l].rearrange("(k p) n -> p k n", p=P), k, n) for name, n, k in ws]
            else:
                return []
            v = w.rearrange("(k p) n -> p k n", p=P)
            return [(v[:, ks[i]:ks[i + 1], c0:c0 + n], ks[i + 1] - ks[i], n) for i in range(2)]

        @block.sync
        def _(sp):
            for dst, src in CONSTS:
                sp.dma_start(dst, src).then_inc(consts_in, 16)
            xt = [a["ctx"][0, 0:P, :], a["ctx"][0, P:2 * P, :], a["x"][0, 0:P, :], a["x"][0, P:2 * P, :]]
            for t in range(TILES):
                sp.dma_start(X[:, t, :], xt[t]).then_inc(x_in, 16)
            n = 0
            for stage in PLAN:
                for src, k, cols in pieces(stage):
                    if n >= WSLOTS:
                        sp.wait_ge(piece_used, n - WSLOTS + 1)
                    sp.dma_start(WT[:, n % WSLOTS, 0:k, 0:cols], src).then_inc(piece_in[n % WSLOTS], 16)
                    n += 1
                if stage == ("close", 4):
                    sp.wait_ge(xn_ready, FINAL_GAIN_AFTER)
                    sp.dma_start(X[:, 0, :], a["final_norm_g"].partition_broadcast(P)).then_inc(fg_in, 16)
                if stage[0] == "last":
                    t = stage[1]
                    sp.wait_ge(y_ready, t + 1)
                    sp.dma_start(out[0, t * P:(t + 1) * P, :], X[:, 2 + t, :]).then_inc(stored, 16)
            sp.wait_ge(stored, 32)

        @block.gpsimd
        def _(pool):
            def unit(b, u, par, fixed):
                n = u + b * (SLOTS // UNIT)

                def wait(s, v):
                    if not fixed:
                        pool.wait_ge(s, v)
                        pool.sem_inc(pool_step, 1)
                    elif v > 0:
                        pool.wait_ge(s, v)

                wait(used_pe, n * 4 - 3)
                at = bass.ds(u * UNIT, UNIT) if not fixed else slice(u * UNIT, (u + 1) * UNIT)
                pool.tensor_copy(FIX[:, par, :], IDX[:, b % HB, at]).then_inc(fix_set, 1)
                wait(fix_set, n + 1)
                for j in range(UNIT):
                    wait(used_dve if j % 2 else used_pe, n * 4 + j // 2 - 3)
                    pool.indirect_dma_start(
                        out=EXPERT[:, j, :], out_offset=None, in_=a["peer_uv"],
                        in_offset=bass.IndirectOffsetOnAxis(ap=FIX[:, par, j:j + 1], axis=0),
                    ).then_inc(landed[j], 16)

            for b in range(6):
                l, t = block_home(b)
                heads_before = PH * (b // 2)
                if b in (0, 4):
                    for u in range(SLOTS // UNIT):
                        pool.wait_ge(idx_ready[t % 2], heads_before + u // 2 + 1)
                        unit(b, u, u % 2, True)
                else:
                    pool.wait_ge(idx_ready[t % 2], heads_before + PH)
                    with pool.Fori(0, SLOTS // UNIT // 2) as pair:
                        for par in range(2):
                            unit(b, pair * 2 + par, par, False)

        @block.tensor
        def _(pe):
            tick = Ticks()
            ra, rb = Ring(banks_a), Ring(banks_b)
            npiece = [0]
            owed = []

            def release():
                while owed:
                    s, n, count = owed.pop()
                    pe.wait_ge(s, n)
                    pe.sem_inc(piece_used, count)

            def fill_a():
                bank, n = ra.next()
                if n > NA:
                    pe.wait_ge(emptied_a, n - NA)
                return bank

            def fill_b():
                bank, n = rb.next()
                if n > NB:
                    pe.wait_ge(emptied_b, n - NB)
                return bank

            def piece():
                n = npiece[0]
                npiece[0] += 1
                pe.wait_ge(piece_in[n % WSLOTS], 16 * (n // WSLOTS + 1))
                return WT[:, n % WSLOTS, :, :]

            def turn_tiles(bank, srcs, rows):
                for i, s in enumerate(srcs):
                    last = nc.tensor.transpose(bank[0:rows, i * P:(i + 1) * P], s, IDN[:, :])
                return last

            def consts(_):
                pe.wait_ge(consts_in, CONSTS_ALL)
                bank = fill_a()
                nc.tensor.transpose(bank[:, 0:ROWS], ROW, IDN[0:ROWS, 0:ROWS])
                nc.tensor.transpose(bank[:, P:P + 2 * MODS], BROW, IDN[0:2 * MODS, 0:2 * MODS]).then_inc(filled_a, 1)
                bank = fill_b()
                turn_tiles(bank, [SK[:, i, :] for i in range(4)], P).then_inc(filled_b, 1)

            def ada(stage):
                _, l, n = stage
                if n == 0:
                    pe.wait_ge(silu_done, 1)
                bank = fill_b()
                for half in range(2):
                    w = piece()
                    for k in range(4):
                        last = nc.tensor.matmul(bank[0:2, :], ST[:, :, 4 * half + k], w[:, k, :],
                                                start=(half + k == 0), stop=(half == 1 and k == 3))
                        if half == 0 and k == 3:
                            last.then_inc(piece_used, 1)
                        if half == 0 and k == 1:
                            release()
                last.then_inc(filled_b, 1)
                owed.append((filled_b, rb.n, 1))

            def adat(stage):
                n = stage[2]
                pe.wait_ge(mrow_ready, tick("mrow"))
                bank = fill_a()
                for k in range(4):
                    last = nc.tensor.transpose(bank[:, 2 * k:2 * k + 2], MROW[:, n % 2, k * P:(k + 1) * P], IDN[0:2, 0:2])
                last.then_inc(filled_a, 1)

            def norm(stage):
                pe.wait_ge(xn_ready, tick("norm"))
                for half in range(2):
                    bank = fill_b()
                    turn_tiles(bank, [XN[:, stage[3], (4 * half + k) * P:(4 * half + k + 1) * P] for k in range(4)], P)\
                        .then_inc(filled_b, 1)
                held["ht", stage[3]] = rb.n

            def back(stage):
                t = stage[3]
                pe.wait_ge(emptied_b, held["ht", t])
                for half in range(2):
                    bank = fill_a()
                    turn_tiles(bank, [HT[:, 4 * half + k, t * P:(t + 1) * P] for k in range(4)], P).then_inc(filled_a, 1)

            def product(stage):
                kind, l, g, name, ts, half = stage
                n = CHUNKS[name][1] if kind == "in" else W
                if half == 0:
                    if kind == "out":
                        gate_rows()
                    pe.wait_ge(emptied_b, rb.n)
                    held["banks"] = [fill_a() for t in ts]
                    held["fills"] = ra.n
                w = piece()
                for t, bank in zip(ts, held["banks"]):
                    for k in range(4):
                        last = nc.tensor.matmul(bank[:, 0:n], HT[:, 4 * half + k, t * P:(t + 1) * P], w[:, k, 0:n],
                                                start=(half + k == 0), stop=(half == 1 and k == 3))
                        if half == 1 and k == 3:
                            last.then_inc(filled_a, 1)
                        elif k == 3 and t == ts[-1]:
                            last.then_inc(piece_used, 1)
                        if t == ts[0] and k == 1:
                            release()
                if half == 1:
                    owed.append((filled_a, held["fills"], 1))

            def gate_rows():
                pe.wait_ge(gd_ready, tick("gd"))
                bank = fill_a()
                for k in range(4):
                    last = nc.tensor.matmul(bank[:, k * P:(k + 1) * P], ONES[:, :], GD[:, k, :], start=True, stop=True)
                last.then_inc(filled_a, 1)

            def up(stage):
                _, l, g, what, ts = stage
                pe.wait_ge(emptied_b, rb.n)
                k0, kn, n = {"q": (0, 3, 512), "r": (0, 3, 256), "k": (3, 2, 512), "v": (3, 2, 512)}[what]
                w = piece()
                for t in ts:
                    bank = fill_a()
                    for k in range(kn):
                        last = nc.tensor.matmul(bank[:, 0:n], HT[:, k0 + k, t * P:(t + 1) * P], w[:, k, 0:n],
                                                start=(k == 0), stop=(k == kn - 1))
                        if k == kn - 1:
                            last.then_inc(filled_a, 1)
                        if t == ts[0] and k == 0:
                            release()
                owed.append((filled_a, ra.n, 1))

            def turn(stage):
                _, l, g, what, ts = stage
                for t in ts:
                    pe.wait_ge(tmp_ready, tick("tmp"))
                    if what in ("q", "k"):
                        src = ASM[:, (2 if what == "k" else 0) + t, :, :]
                        for half in range(2):
                            bank = fill_b()
                            turn_tiles(bank, [src[:, 4 * half + h, :] for h in range(4)], MQ).then_inc(filled_b, 1)
                    else:
                        src = TMP[:, tmp_slot(what) + t, :]
                        cols = {"qd": 4, "kd": 4, "cq": 3, "kv": 2}[what]
                        bank = fill_b()
                        turn_tiles(bank, [src[:, k * P:(k + 1) * P] for k in range(cols)], P).then_inc(filled_b, 1)

            def attn(stage):
                _, l, g, t, i = stage
                keys = 2 * P if g == CTX else 4 * P
                if i == -1:
                    pe.wait_ge(emptied_b, rb.n)
                    pe.wait_ge(emptied_a, ra.n)
                if i + 1 < MH + DH:
                    h = i + 1
                    for c in range(1 if h < MH else 2):
                        bank = fill_b()
                        if h < MH:
                            q, k = QTM[:, h, t * P:(t + 1) * P], KTM[:, h, 0:keys]
                        else:
                            q = QTD[64 * c:64 * c + 64, h - MH, t * P:(t + 1) * P]
                            k = KTD[64 * c:64 * c + 64, h - MH, 0:keys]
                        nc.tensor.matmul(bank[:, 0:keys], q, k, start=True, stop=True).then_inc(filled_b, 1)
                if 0 <= i < MH + DH:
                    bank = fill_a()
                    if i < MH:
                        pe.wait_ge(exp_ready, tick.so_far("heads") + 1)
                    else:
                        pe.wait_ge(mixed_ready, tick("mixed"))
                    tick("heads")
                    turn_tiles(bank, [PR[:, i % 2, 0, k * P:(k + 1) * P] for k in range(keys // P)], P)\
                        .then_inc(filled_a, 1)
                    pt_fill.append(ra.n)
                if i >= 1:
                    h = i - 1
                    bank = fill_a()
                    pe.wait_ge(emptied_a, pt_fill.pop(0))
                    v = VM[:, :, h * MD:(h + 1) * MD] if h < MH else VD[:, :, (h - MH) * P:(h - MH + 1) * P]
                    n = MD if h < MH else P
                    for k in range(keys // P):
                        last = nc.tensor.matmul(bank[:, 0:n], PT[:, h % 2, k * P:(k + 1) * P], v[:, k, :],
                                                start=(k == 0), stop=(k == keys // P - 1))
                    last.then_inc(filled_a, 1)

            pt_fill = []
            held = {}

            def heads(stage):
                pe.wait_ge(o_ready, tick("o"))
                for half in range(2):
                    bank = fill_b()
                    turn_tiles(bank, [O[:, (4 * half + k) * P:(4 * half + k + 1) * P] for k in range(4)], P)\
                        .then_inc(filled_b, 1)

            def pick_(stage):
                _, l, g, h = stage
                if h == 0:
                    pe.wait_ge(emptied_b, rb.n)
                if h < PH:
                    if h % 2 == 0:
                        release()
                        held["w"] = [piece(), piece()]
                    for c in range(2):
                        bank = fill_b()
                        for k in range(KD):
                            at = (h % 2) * 256 + c * P
                            last = nc.tensor.matmul(bank[:, 0:2 * P], held["w"][k // 4][:, k % 4, at:at + P], HT[:, k, :],
                                                    start=(k == 0), stop=(k == KD - 1))
                        last.then_inc(filled_b, 1)
                        held[h, c] = rb.n
                    if h % 2 == 1:
                        owed.append((filled_b, rb.n, 2))
                if h >= 1:
                    pe.wait_ge(emptied_b, held[h - 1, 1])
                    for t in range(2):
                        bank = fill_a()
                        for c in range(2):
                            last = nc.tensor.matmul(bank[:, c * P:(c + 1) * P], QP[:, (h - 1) % 2, c, t * P:(t + 1) * P],
                                                    SKT[:, 2 * l + c, :], start=True, stop=True)
                        last.then_inc(filled_a, 1)

            def apply(no, j, first=False, last_one=False):
                pe.wait_ge(diag_ready, no + 1)
                for n in range(2):
                    ins = nc.tensor.matmul(VSUM[n][:, :], DIAG[:, j // 2 % 2, :], EXPERT[:, j, D + n * W:D + (n + 1) * W],
                                           start=first, stop=last_one)
                ins.then_inc(used_pe, 1)

            def quads(stage):
                _, b, q0, q1 = stage
                release()
                for kind, v0, v1 in parts_of(q0, q1):
                    if kind == "loop":
                        with pe.Fori(v0 // 4, v1 // 4) as four:
                            for k in range(8):
                                apply(four * 8 + (b * SLOTS // 2 + k), 2 * k % RING)
                    else:
                        if v0 == 0 and b > 0:
                            pe.wait_ge(vsum_read, 2 * b)
                        for k in range(2):
                            apply(slot_no(b, v0) // 2 + k, (v0 % 2) * 4 + 2 * k, first=(v0 + k == 0),
                                  last_one=(v0 == QUADS - 1 and k == 1))

            def close(stage):
                for n in range(2):
                    gate_rows()

            do = {"consts": consts, "ada": ada, "adat": adat, "norm": norm, "back": back, "in": product, "out": product,
                  "up": up, "turn": turn, "attn": attn, "heads": heads, "pick": pick_, "quads": quads, "close": close}
            for stage in PLAN:
                if stage[0] in do:
                    do[stage[0]](stage)

        @block.scalar
        def _(act):
            tick = Ticks()
            rb = Ring(banks_b)
            steps = [0]

            def link(ins):
                steps[0] += 1
                ins.then_inc(act_step, 1)
                act.wait_ge(act_step, steps[0])

            def from_b():
                bank, n = rb.next()
                act.wait_ge(filled_b, n)
                return bank

            def consts(_):
                bank = from_b()
                nc.scalar.copy(SKT[:, :, :].rearrange("p i n -> p (i n)"), bank[:, :]).then_inc(emptied_b, 1)
                act.wait_ge(cols_set, 1)
                nc.scalar.activation(ST[:, :, :].rearrange("p c k -> p (c k)"), COL[:, 0, 0:2 * KD], ACT.Silu)\
                    .then_inc(silu_done, 1)
                act.wait_ge(lam_sums, 2 * DEPTH)
                nc.scalar.activation(LE[:, :], LS[:, :], ACT.Exp).then_inc(lam_exps, 1)

            def ada(stage):
                bank = from_b()
                nc.scalar.copy(MROW[:, stage[2] % 2, :], bank[0:2, :]).then_inc(emptied_b, 1)
                act.wait_ge(emptied_b, rb.n)
                act.sem_inc(mrow_ready, 1)

            def mean_square(tile, place):
                link(nc.scalar.activation(place, X[:, tile, :], ACT.Square, accum_out=NS[:, :]))
                nc.scalar.activation(NQ[:, :], NS[:, :], ACT.Sqrt, scale=1.0 / D, bias=EPST[:, :]).then_inc(root_ready, 1)

            def stat(stage):
                _, l, g, t, which = stage
                tile = 2 * g + t
                if which == 1 and l == 0:
                    act.wait_ge(x_in, 16 * TILES)
                else:
                    act.wait_ge(x_ready[tile], 2 * l + (which == 2))
                mean_square(tile, XN[:, t, :])
                act.wait_ge(rs_ready, tick("norm"))
                nc.scalar.activation(XN[:, t, :], X[:, tile, :], ACT.Copy, scale=NR[:, :]).then_inc(xn_ready, 1)

            def norm(stage):
                _, l, g, t, which = stage
                act.wait_ge(mod_ready, 2 * l + which)
                at = (1 if which == 1 else 4) * KD
                m = 1 - g
                for half in range(2):
                    bank = from_b()
                    for k in range(4):
                        j = at + 4 * half + k
                        last = nc.scalar.activation(HT[:, 4 * half + k, t * P:(t + 1) * P], bank[:, k * P:(k + 1) * P],
                                                    ACT.Identity, scale=MOD[:, l, j, m:m + 1],
                                                    bias=MOD[:, l, j - KD, m:m + 1])
                    last.then_inc(emptied_b, 1)

            def root(stage):
                _, l, g, what, ts = stage
                act.wait_ge(ss_ready, tick("ss"))
                at = slice(root_at(what, ts[0]), root_at(what, ts[-1]) + 1)
                nc.scalar.activation(SQ[:, at], SS[:, at], ACT.Sqrt, scale=1.0 / (QR if what == "cq" else KVR),
                                     bias=EPST[:, :]).then_inc(sq_ready, 1)

            def turn(stage):
                _, l, g, what, ts = stage
                for t in ts:
                    keys = slice((2 * g + t) * P, (2 * g + t + 1) * P)
                    mine = slice(t * P, (t + 1) * P)
                    if what in ("q", "k"):
                        dst, at = (QTM, mine) if what == "q" else (KTM, keys)
                        for half in range(2):
                            bank = from_b()
                            nc.scalar.copy(dst[:, 4 * half:4 * half + 4, at],
                                           bank[0:MQ, :].rearrange("p (h n) -> p h n", h=4)).then_inc(emptied_b, 1)
                    elif what in ("qd", "kd"):
                        dst, at = (QTD, mine) if what == "qd" else (KTD, keys)
                        bank = from_b()
                        nc.scalar.copy(dst[:, :, at], bank[:, :].rearrange("p (h n) -> p h n", h=4))\
                            .then_inc(emptied_b, 1)
                    else:
                        k0, kn, r = (0, 3, R_QN + 3 * l) if what == "cq" else (3, 2, R_KN + 2 * l)
                        bank = from_b()
                        for k in range(kn):
                            last = nc.scalar.activation(HT[:, k0 + k, mine], bank[:, k * P:(k + 1) * P], ACT.Copy,
                                                        scale=COL[:, 0, r + k:r + k + 1])
                        last.then_inc(emptied_b, 1)

            def attn(stage):
                _, l, g, t, i = stage
                keys = 2 * P if g == CTX else 4 * P
                h = i + 1
                if h < MH + DH:
                    act.wait_ge(negmax_ready, tick("negmax"))
                    for c in range(1 if h < MH else 2):
                        bank = from_b()
                        ins = nc.scalar.activation(PR[:, h % 2, c, 0:keys], bank[:, 0:keys], ACT.Exp,
                                                   bias=NM[:, h % 2, c:c + 1], scale=SC_M if h < MH else SC_D,
                                                   accum_out=SUM[:, h % 2, c:c + 1])
                        ins.then_inc(emptied_b, 1)
                    act.wait_ge(emptied_b, rb.n)
                    act.sem_inc(exp_ready, 1)

            def hnorm(stage):
                act.wait_ge(ss_ready, tick("ss"))
                nc.scalar.activation(SQ[:, :], SS[:, :], ACT.Sqrt, scale=1.0 / P, bias=EPST[:, :]).then_inc(sq_ready, 1)

            def heads(stage):
                _, l, g, t = stage
                for half in range(2):
                    bank = from_b()
                    src = bank[:, :].rearrange("p (h n) -> p h n", h=4)
                    dst = HT[:, 4 * half:4 * half + 4, t * P:(t + 1) * P]
                    if half == 0:
                        nc.scalar.copy(dst, src).then_inc(emptied_b, 1)
                    else:
                        nc.scalar.activation(dst, src, ACT.Copy, scale=SUBG[:, l:l + 1]).then_inc(emptied_b, 1)

            def pick_(stage):
                _, l, g, h = stage
                if h < PH:
                    for c in range(2):
                        bank = from_b()
                        nc.scalar.copy(QP[:, h % 2, c, :], bank[:, 0:2 * P]).then_inc(emptied_b, 1)
                if h >= 1:
                    for t in range(2):
                        act.wait_ge(top_ready, tick("top"))
                        nc.scalar.activation(TE[:, t, :], TS[:, t, :], ACT.Exp, bias=NT[:, t:t + 1],
                                             accum_out=TSUM[:, t:t + 1]).then_inc(topexp_ready, 1)

            def weigh(no, pair, j, gate):
                one = slice(j % 4, j % 4 + 1)
                act.wait_ge(dots_ready, no + 1)
                nc.scalar.activation(GEL[:, one], DOT[:, one], ACT.Gelu).then_inc(gelu_ready, 1)
                act.wait_ge(gelu_ready, no + 1)
                nc.scalar.activation(WEI[:, one], GEL[:, one], ACT.Copy, scale=gate).then_inc(wei_ready, 1)
                if j % 2 == 0:
                    act.wait_ge(wei_ready, no + 1)
                    if not isinstance(pair, int) or pair >= 2:
                        act.wait_ge(used_pe, pair - 1)
                    nc.scalar.activation(DIAG[:, j // 2 % 2, :], IDN[:, :], ACT.Copy, scale=WEI[:, one])\
                        .then_inc(diag_ready, 1)

            def quads(stage):
                _, b, q0, q1 = stage
                for kind, v0, v1 in parts_of(q0, q1):
                    if kind == "loop":
                        with act.Fori(v0 // 4, v1 // 4) as four:
                            for i in range(16):
                                weigh(four * 16 + (b * SLOTS + i), four * 8 + (b * SLOTS + i) // 2, i % RING,
                                      GATE[:, b % HB, bass.ds(four * 16 + i, 1)])
                    else:
                        for i in range(4):
                            no = slot_no(b, v0, i)
                            weigh(no, no // 2, no % RING, GATE[:, b % HB, v0 * 4 + i:v0 * 4 + i + 1])

            def last_(stage):
                t = stage[1]
                act.wait_ge(x_ready[2 + t], 4)
                mean_square(2 + t, XN[:, t, :])

            do = {"consts": consts, "ada": ada, "stat": stat, "norm": norm, "root": root, "turn": turn, "attn": attn,
                  "hnorm": hnorm, "heads": heads, "pick": pick_, "quads": quads, "last": last_}
            for stage in late(PLAN):
                if stage[0] in do:
                    do[stage[0]](stage)

        @block.vector
        def _(dve):
            tick = Ticks()
            ra, rb = Ring(banks_a), Ring(banks_b)
            steps = [0]

            def link(ins):
                steps[0] += 1
                ins.then_inc(dve_step, 1)
                dve.wait_ge(dve_step, steps[0])

            def from_a():
                bank, n = ra.next()
                dve.wait_ge(filled_a, n)
                return bank

            def tt(o, x, y, op):
                return nc.vector.tensor_tensor(o, x, y, op)

            def consts(_):
                nc.vector.memset(EPST[:, :], EPS)
                nc.vector.memset(ONES[:, :], 1.0)
                dve.wait_ge(consts_in, CONSTS_ALL)
                bank = from_a()
                nc.vector.tensor_copy(COL[:, 0, 0:ROWS], bank[:, 0:ROWS]).then_inc(cols_set, 1)
                dve.wait_ge(cols_set, 1)
                link(nc.vector.tensor_copy(COL[:, 1, :], bank[:, P:P + 2 * MODS]))
                nc.vector.tensor_scalar(SUBG[:, 0:1], COL[:, 0, R_SN:R_SN + 1], 1.0 - lam_init(0), None, ALU.mult)
                nc.vector.tensor_scalar(SUBG[:, 1:2], COL[:, 0, R_SN + 1:R_SN + 2], 1.0 - lam_init(1), None, ALU.mult)\
                    .then_inc(emptied_a, 1)
                rb.next()
                for l in range(DEPTH):
                    for i in range(2):
                        nc.vector.tensor_tensor_reduce(out=LT[:, 2 * l + i, :], in0=LM[:, l, 2 * i, :], in1=LM[:, l, 2 * i + 1, :],
                                                       scale=1.0, scalar=0.0, op0=ALU.mult, op1=ALU.add,
                                                       accum_out=LS[:, 2 * l + i:2 * l + i + 1]).then_inc(lam_sums, 1)
                dve.wait_ge(lam_exps, 1)
                for l in range(DEPTH):
                    link(tt(LAM[:, l:l + 1], LE[:, 2 * l:2 * l + 1], LE[:, 2 * l + 1:2 * l + 2], ALU.subtract))
                    link(nc.vector.tensor_scalar(LAM[:, l:l + 1], LAM[:, l:l + 1], lam_init(l), None, ALU.add))

            def ada(stage):
                rb.next()

            def adat(stage):
                _, l, n = stage
                bank = from_a()
                tt(MOD[:, l, 4 * n:4 * n + 4, :], bank[:, 0:8].rearrange("p (k c) -> p k c", c=2),
                   COL[:, 1, l * MODS + 4 * n:l * MODS + 4 * n + 4].unsqueeze(2).to_broadcast([P, 4, 2]),
                   ALU.add).then_inc(emptied_a, 1)

            def mod(stage):
                _, l, which = stage
                dve.wait_ge(emptied_a, ra.n)
                at, r = (KD, R_NA) if which == 1 else (4 * KD, R_NF)
                m = MOD[:, l, at:at + KD, :]
                link(nc.vector.tensor_scalar(m, m, 1.0, None, ALU.add))
                tt(m, m, COL[:, 0, r + l * KD:r + (l + 1) * KD].unsqueeze(2).to_broadcast([P, KD, 2]), ALU.mult)\
                    .then_inc(mod_ready, 1)
                dve.wait_ge(mod_ready, 2 * l + which)

            def invert():
                dve.wait_ge(root_ready, tick("norm"))
                nc.vector.reciprocal(NR[:, :], NQ[:, :]).then_inc(rs_ready, 1)
                dve.wait_ge(rs_ready, tick.so_far("norm"))

            def stat(stage):
                invert()

            def norm(stage):
                rb.next()
                rb.next()

            def back(stage):
                _, l, g, t = stage
                b = blocks_of(l, g)[t]
                for half in range(2):
                    bank = from_a()
                    nc.vector.tensor_copy(H2[:, b % HB, half * W:(half + 1) * W], bank[:, :]).then_inc(emptied_a, 1)
                dve.wait_ge(emptied_a, ra.n)

            def rotate(dst, src, table, heads, width):
                def table_at(s, odd):
                    v = table[:, s, :].rearrange("p (n two) -> p n two", two=2)[:, :, odd]
                    return v.unsqueeze(1).to_broadcast([P, heads, width // 2])

                r = ROT[:, 0:heads * width].rearrange("p (h n) -> p h n", h=heads)
                r2 = r.rearrange("p h (n two) -> p h n two", two=2)
                s2 = src.rearrange("p h (n two) -> p h n two", two=2)
                tt(r2[:, :, :, 0], s2[:, :, :, 1], table_at(1, 0), ALU.mult)
                tt(r2[:, :, :, 1], s2[:, :, :, 0], table_at(1, 1), ALU.mult)
                link(tt(dst, src, table[:, 0, :].unsqueeze(1).to_broadcast([P, heads, width]), ALU.mult))
                return tt(dst, dst, r, ALU.add)

            def roots(at):
                dve.wait_ge(sq_ready, tick("sq"))
                link(nc.vector.reciprocal(RS[:, at], SQ[:, at]))

            def in_(stage):
                _, l, g, what, ts, half = stage
                if half == 0:
                    return
                if what in pend_free and pend_free[what] in turned:
                    dve.wait_ge(filled_b, turned[pend_free[what]])
                for t in ts:
                    bank = from_a()
                    tile = 2 * g + t
                    tmp = TMP[:, (0 if what == "vd" else tmp_slot(what)) + t, :]
                    if what == "vd":
                        nc.vector.tensor_copy(VD[:, tile, :], bank[:, :]).then_inc(emptied_a, 1)
                    elif what in ("qd", "kd"):
                        if g == LAT:
                            link(rotate(tmp.rearrange("p (h n) -> p h n", n=DD),
                                        bank[:, :].rearrange("p (h n) -> p h n", n=DD), ROPD[:, t, :, :], 2 * DH, DD))
                            free_a()
                            dve.sem_inc(tmp_ready, 1)
                        else:
                            link(nc.vector.tensor_copy(tmp, bank[:, :]))
                            free_a()
                            dve.sem_inc(tmp_ready, 1)
                    else:
                        n = QR if what == "cq" else KVR
                        link(nc.vector.tensor_copy(tmp[:, 0:n], bank[:, 0:n]))
                        if what == "kv":
                            kr = KR[:, t, :].unsqueeze(1)
                            src = bank[:, n:n + RD].unsqueeze(1)
                            if g == LAT:
                                link(rotate(kr, src, ROPM[:, t, :, :], 1, RD))
                            else:
                                link(nc.vector.tensor_copy(kr, src))
                        free_a()
                        ins = nc.vector.tensor_tensor_reduce(out=ROT[:, 0:n], in0=tmp[:, 0:n], in1=tmp[:, 0:n], scale=1.0,
                                                             scalar=0.0, op0=ALU.mult, op1=ALU.add,
                                                             accum_out=SS[:, root_at(what, t):root_at(what, t) + 1])
                        if t != ts[-1]:
                            link(ins)
                        else:
                            ins.then_inc(ss_ready, 1)
                            dve.wait_ge(ss_ready, tick("ss"))

            def free_a():
                dve.sem_inc(emptied_a, 1)

            pend_free = {"cq": "qd", "kv": "kd"}
            turned = {}

            def root(stage):
                _, l, g, what, ts = stage
                roots(slice(root_at(what, ts[0]), root_at(what, ts[-1]) + 1))
                for t in ts:
                    tmp = TMP[:, tmp_slot(what) + t, 0:QR if what == "cq" else KVR]
                    nc.vector.tensor_scalar(tmp, tmp, RS[:, root_at(what, t):root_at(what, t) + 1], None, ALU.mult)\
                        .then_inc(tmp_ready, 1)

            def turn(stage):
                _, l, g, what, ts = stage
                for t in range(len(ts) * (2 if what in ("q", "k") else 1)):
                    rb.next()
                turned[what] = rb.n
                if what == "kv":
                    turned.clear()

            def up(stage):
                _, l, g, what, ts = stage
                if what in ("q", "k", "v"):
                    for t in ts:
                        bank = from_a()
                        tile = 2 * g + t
                        if what == "v":
                            nc.vector.tensor_copy(VM[:, tile, :], bank[:, :]).then_inc(emptied_a, 1)
                            continue
                        asm = ASM[:, (2 if what == "k" else 0) + t, :, :]
                        nc.vector.tensor_copy(asm[:, :, 0:MD], bank[:, :].rearrange("p (h n) -> p h n", n=MD))\
                            .then_inc(emptied_a, 1)
                        if what == "k":
                            nc.vector.tensor_copy(asm[:, :, MD:MQ], KR[:, t, :].unsqueeze(1).to_broadcast([P, MH, RD]))\
                                .then_inc(tmp_ready, 1)
                else:
                    for t in ts:
                        bank = from_a()
                        asm = ASM[:, t, :, :]
                        src = bank[:, 0:MH * RD].rearrange("p (h n) -> p h n", n=RD)
                        if g == LAT:
                            link(rotate(asm[:, :, MD:MQ], src, ROPM[:, t, :, :], MH, RD))
                        else:
                            link(nc.vector.tensor_copy(asm[:, :, MD:MQ], src))
                        free_a()
                        dve.sem_inc(tmp_ready, 1)

            def attn(stage):
                _, l, g, t, i = stage
                keys = 2 * P if g == CTX else 4 * P
                h = i + 1
                if h < MH + DH:
                    maps = 1 if h < MH else 2
                    for c in range(maps):
                        bank, n = rb.next()
                        dve.wait_ge(filled_b, n)
                        ins = nc.vector.reduce_max(MX[:, h % 2, c:c + 1], bank[:, 0:keys], AX_X)
                    link(ins)
                    nc.vector.tensor_scalar(NM[:, h % 2, 0:maps], MX[:, h % 2, 0:maps], -(SC_M if h < MH else SC_D), None,
                                            ALU.mult).then_inc(negmax_ready, 1)
                if 0 <= i < MH + DH:
                    maps = 1 if i < MH else 2
                    dve.wait_ge(exp_ready, tick("exp"))
                    link(nc.vector.reciprocal(INV[:, i % 2, 0:maps], SUM[:, i % 2, 0:maps]))
                    if i >= MH:
                        link(tt(INV[:, i % 2, 1:2], INV[:, i % 2, 1:2], LAM[:, l:l + 1], ALU.mult))
                        p0, p1 = PR[:, i % 2, 0, 0:keys], PR[:, i % 2, 1, 0:keys]
                        link(nc.vector.tensor_scalar(p1, p1, INV[:, i % 2, 1:2], None, ALU.mult))
                        nc.vector.scalar_tensor_tensor(out=p0, in0=p0, scalar=INV[:, i % 2, 0:1], in1=p1, op0=ALU.mult,
                                                       op1=ALU.subtract).then_inc(mixed_ready, 1)
                    bank = from_a()
                    nc.vector.tensor_copy(PT[:, i % 2, 0:keys], bank[:, 0:keys]).then_inc(emptied_a, 1)
                if i >= 1:
                    h = i - 1
                    bank = from_a()
                    if h < MH:
                        nc.vector.tensor_scalar(O[:, h * MD:(h + 1) * MD], bank[:, 0:MD], INV[:, h % 2, 0:1], None,
                                                ALU.mult).then_inc(emptied_a, 1)
                    else:
                        at = MH * MD + (h - MH) * P
                        nc.vector.tensor_copy(O[:, at:at + P], bank[:, 0:P]).then_inc(emptied_a, 1)

            def hnorm(stage):
                dve.wait_ge(emptied_a, ra.n)
                od = O[:, MH * MD:D].rearrange("p (h n) -> p h n", h=DH)
                sq = PT[:, 0, :].rearrange("p (h n) -> p h n", h=DH)
                link(tt(sq, od, od, ALU.mult))
                nc.vector.tensor_reduce(SS[:, :], sq, AX_X, ALU.add).then_inc(ss_ready, 1)
                tick("ss")
                roots(slice(0, 4))
                tt(od, od, RS[:, :].unsqueeze(2).to_broadcast([P, DH, P]), ALU.mult).then_inc(o_ready, 1)

            def heads(stage):
                rb.next()
                rb.next()

            def diagonals(l, g, which, n):
                at = (2 if which == 1 else 5) * KD + 4 * n
                m = 1 - g
                tt(GD[:, :, :], IDN[:, :].unsqueeze(1).to_broadcast([P, 4, P]),
                   MOD[:, l, at:at + 4, m:m + 1].to_broadcast([P, 4, P]), ALU.mult).then_inc(gd_ready, 1)

            def gates(stage):
                _, l, g, n = stage
                diagonals(l, g, 1, n)

            def out_(stage):
                _, l, g, n, ts, half = stage
                if half == 0:
                    return
                bank = from_a()
                nc.vector.tensor_copy(GROW, bank[:, :]).then_inc(emptied_a, 1)
                dve.wait_ge(emptied_a, ra.n)
                for t in range(2):
                    bank = from_a()
                    x = X[:, 2 * g + t, n * W:(n + 1) * W]
                    tt(YT[:, t, :], bank[:, :], GROW, ALU.mult).then_inc(emptied_a, 1)
                    dve.wait_ge(emptied_a, ra.n)
                    ins = tt(x, x, YT[:, t, :], ALU.add)
                    if n == 1:
                        ins.then_inc(x_ready[2 * g + t], 1)

            def pick_(stage):
                _, l, g, h = stage
                if h < PH:
                    rb.next()
                    rb.next()
                if h == 0:
                    return
                h -= 1
                for t in range(2):
                    b = blocks_of(l, g)[t]
                    bank = from_a()
                    for c in range(2):
                        s = bank[:, c * P:(c + 1) * P]
                        link(nc.vector.max(SV[:, c, 0:8], s))
                        nc.vector.max_index(SI[:, c, 0:8], SV[:, c, 0:8], s)
                        link(nc.vector.match_replace(WK[:, c, :], SV[:, c, 0:8], s, LOWEST))
                        link(nc.vector.max(SV[:, c, 8:16], WK[:, c, :]))
                        link(nc.vector.max_index(SI[:, c, 8:16], SV[:, c, 8:16], WK[:, c, :]))
                    free_a()
                    nc.vector.tensor_copy(SIF[:, :, :], SI[:, :, :])
                    cand = CAND.rearrange("p (i j) -> p i j", i=TOPK)
                    link(tt(cand, SV[:, 0, :].unsqueeze(2).to_broadcast([P, TOPK, TOPK]),
                            SV[:, 1, :].unsqueeze(1).to_broadcast([P, TOPK, TOPK]), ALU.add))
                    link(nc.vector.max(TS[:, t, 0:8], CAND))
                    nc.vector.max_index(POS[:, 0:8], TS[:, t, 0:8], CAND)
                    link(nc.vector.match_replace(CANW, TS[:, t, 0:8], CAND, LOWEST))
                    link(nc.vector.max(TS[:, t, 8:16], CANW))
                    nc.vector.tensor_scalar(NT[:, t:t + 1], TS[:, t, 0:1], -1.0, None, ALU.mult).then_inc(top_ready, 1)
                    link(nc.vector.max_index(POS[:, 8:16], TS[:, t, 8:16], CANW))
                    nc.vector.tensor_scalar(AB[:, 0, :], POS[:, :], 4, None, ALU.logical_shift_right)
                    link(nc.vector.tensor_scalar(AB[:, 1, :], POS[:, :], 15, None, ALU.bitwise_and))
                    link(nc.vector.tensor_copy(ABF[:, :, :], AB[:, :, :]))
                    for c in range(2):
                        tt(HOT[:, c], ABF[:, c, :].unsqueeze(2).to_broadcast([P, TOPK, TOPK]),
                           IOTA[:, :].unsqueeze(1).to_broadcast([P, TOPK, TOPK]), ALU.is_equal).then_inc(dve_step, 1)
                        steps[0] += 1
                    dve.wait_ge(dve_step, steps[0])
                    for c in range(2):
                        ins = tt(HOT[:, c], HOT[:, c], SIF[:, c, :].unsqueeze(1).to_broadcast([P, TOPK, TOPK]), ALU.mult)
                    link(ins)
                    link(nc.vector.tensor_reduce(PICK[:, :, :], HOT, AX_X, ALU.add))
                    at = slice(h * TOPK, (h + 1) * TOPK)
                    link(nc.vector.scalar_tensor_tensor(out=PICK[:, 0, :], in0=PICK[:, 0, :], scalar=float(NK),
                                                        in1=PICK[:, 1, :], op0=ALU.mult, op1=ALU.add))
                    link(nc.vector.tensor_scalar(IDX[:, b % HB, at], PICK[:, 0, :], float(l * NK * NK), None, ALU.add))
                    dve.wait_ge(topexp_ready, tick("topexp"))
                    link(nc.vector.reciprocal(TINV[:, t:t + 1], TSUM[:, t:t + 1]))
                    nc.vector.tensor_scalar(GATE[:, b % HB, at], TE[:, t, :], TINV[:, t:t + 1], None, ALU.mult)\
                        .then_inc(idx_ready[t], 1)
                    dve.wait_ge(idx_ready[t], 8 * (b // 2) + h + 1)

            def dot(b, j, landing):
                dve.wait_ge(landed[j], landing * 16)
                nc.vector.tensor_tensor_reduce(out=EXPERT[:, j, 0:D], in0=EXPERT[:, j, 0:D], in1=H2[:, b % HB, :],
                                               scale=1.0, scalar=0.0, op0=ALU.mult, op1=ALU.add,
                                               accum_out=DOT[:, j % 4:j % 4 + 1]).then_inc(dots_ready, 1)

            def apply(no, pair, j):
                dve.wait_ge(wei_ready, no + 1)
                if not isinstance(pair, int) or pair > 0:
                    dve.wait_ge(used_dve, pair)
                nc.vector.scalar_tensor_tensor(out=ACC[:, :], in0=EXPERT[:, j, D:2 * D], scalar=WEI[:, j % 4:j % 4 + 1],
                                               in1=ACC[:, :], op0=ALU.mult, op1=ALU.add).then_inc(used_dve, 1)

            def quads(stage):
                _, b, q0, q1 = stage
                for kind, v0, v1 in parts_of(q0, q1):
                    if kind == "loop":
                        with dve.Fori(v0 // 4, v1 // 4) as four:
                            for i in range(16):
                                dot(b, i % RING, four * 2 + ((b * SLOTS + i) // RING + 1))
                                if i % 2 == 0:
                                    apply(four * 16 + (b * SLOTS + i - 1), four * 8 + (b * SLOTS + i - 2) // 2,
                                          (i - 1) % RING)
                    else:
                        if v0 == 0:
                            nc.vector.memset(ACC[:, :], 0.0).then_inc(acc_zero, 1)
                            dve.wait_ge(acc_zero, b + 1)
                        for i in range(4):
                            no = slot_no(b, v0, i)
                            dot(b, no % RING, no // RING + 1)
                            if i % 2 == 0 and v0 + i > 0:
                                apply(no - 1, (no - 1) // 2, (no - 1) % RING)

            def close(stage):
                b = stage[1]
                l, tile = block_home(b)
                no = slot_no(b + 1, 0)
                apply(no - 1, (no - 1) // 2, RING - 1)
                dve.wait_ge(used_dve, no // 2)
                dve.wait_ge(used_pe, no // 2)
                for n in range(2):
                    half = slice(n * W, (n + 1) * W)
                    diagonals(l, tile // 2, 2, n)
                    tt(ACC[:, half], ACC[:, half], VSUM[n][:, :], ALU.add).then_inc(vsum_read, 1)
                    rows = from_a()
                    dve.wait_ge(vsum_read, 2 * b + n + 1)
                    link(tt(ACC[:, half], ACC[:, half], rows[:, :], ALU.mult))
                    free_a()
                    x = X[:, tile, half]
                    ins = tt(x, x, ACC[:, half], ALU.add)
                    if n == 1:
                        ins.then_inc(x_ready[tile], 1)
                        dve.wait_ge(x_ready[tile], 2 * l + 2)

            def last_(stage):
                t = stage[1]
                invert()
                dve.wait_ge(fg_in, 16)
                x = X[:, 2 + t, :]
                nc.vector.scalar_tensor_tensor(out=x, in0=x, scalar=NR[:, :], in1=X[:, 0, :], op0=ALU.mult,
                                               op1=ALU.mult).then_inc(y_ready, 1)

            do = {"consts": consts, "ada": ada, "adat": adat, "mod": mod, "stat": stat, "norm": norm, "back": back,
                  "in": in_, "out": out_, "gates": gates, "up": up, "root": root, "turn": turn, "attn": attn,
                  "hnorm": hnorm, "heads": heads, "pick": pick_, "quads": quads, "close": close, "last": last_}
            for stage in late(PLAN):
                if stage[0] in do:
                    do[stage[0]](stage)


_INS = ["x", "c", "ctx", "c_ctx", "norm_attn_g", "norm_ffn_g", "w_ada", "b_ada", "w_in", "mla_q_norm_g", "mla_wq_up",
        "mla_wq_rope", "mla_kv_norm_g", "mla_wk_up", "mla_wv_up", "diff_lambda", "diff_subnorm_g", "w_out", "peer_wq",
        "peer_subkeys", "final_norm_g"]


def rope_table(np, width, seq=256, grid=64, base=10000.0):
    quarter = width // 4
    freq = (np.float32(base) ** (-np.arange(quarter, dtype=np.float32) / np.float32(quarter))).astype(np.float32)
    row = np.repeat(np.arange(seq // grid, dtype=np.float32), grid)
    col = np.tile(np.arange(grid, dtype=np.float32), seq // grid)
    ang = np.concatenate([row[:, None] * freq, col[:, None] * freq], axis=-1)
    cos = np.repeat(np.cos(ang), 2, axis=-1)
    sin = np.repeat(np.sin(ang), 2, axis=-1) * np.tile(np.array([-1.0, 1.0], np.float32), width // 2)
    return np.stack([cos, sin], axis=1).astype(np.float32)


def kernel(**inputs):
    import numpy as np
    import concourse.bacc as bacc
    from concourse.bass_utils import run_bass_kernel_spmd

    nc = bacc.Bacc("TRN2", target_bir_lowering=False, num_devices=1)
    host = {n: np.asarray(inputs[n]) for n in _INS}
    u, v = np.asarray(inputs["peer_u"]), np.asarray(inputs["peer_v"])
    host["peer_uv"] = np.concatenate([u, v], axis=-1).reshape(-1, u.shape[-1] + v.shape[-1])
    host["ident"] = np.eye(P, dtype=np.float32)
    host["iota"] = np.arange(TOPK, dtype=np.float32)
    host["rope_mla"] = rope_table(np, RD)
    host["rope_diff"] = rope_table(np, DD)
    arrays, aps = {}, {}
    for name, arr in host.items():
        arr = np.ascontiguousarray(arr)
        arrays[f"in_{name}"] = arr
        aps[name] = nc.dram_tensor(f"in_{name}", arr.shape, mybir.dt.from_np(arr.dtype), kind="ExternalInput").ap()
    out = nc.dram_tensor("out_y", (1, 256, D), F32, kind="ExternalOutput").ap()
    backbone(nc, aps, out)
    got = run_bass_kernel_spmd(nc, [arrays], core_ids=[0])
    return got.results[0]["out_y"]
```

```python
import math
from contextlib import ExitStack

import concourse.bass as bass
from concourse import mybir

F32 = mybir.dt.float32
U32 = mybir.dt.uint32
ALU = mybir.AluOpType
ACT = mybir.ActivationFunctionType
AX_X = mybir.AxisListType.X

P = 128
D = 1024
KD = D // P
DEPTH = 2
TILES = 4
EPS = 1e-6
QR, KVR, RD = 384, 256, 32
MH, MD = 8, 64
MQ = MD + RD
DH, DD = 4, 64
PH, TOPK, NK = 8, 16, 128
SLOTS = PH * TOPK
W = 512
NA = 3
NB = 3
WSLOTS = 4
KP = 2
RING = 8
HB = 3
UNIT = 8
QUADS = SLOTS // 4
BY_PE = 3
AHEAD = 4
BOTH = (0, 1)
CTX, LAT = 0, 1
CHUNKS = {"cq": (0, 384), "kv": (384, 288), "qd": (672, 512), "kd": (1184, 512), "vd": (1696, 512)}
HALVES = ((0, KD // 2), (KD // 2, KD))
SC_M = MQ ** -0.5
SC_D = DD ** -0.5
LOWEST = -3.0e38

R_C, R_CC, R_NA, R_NF, R_QN, R_KN, R_SN = 0, 8, 16, 32, 48, 54, 58
ROWS = 60
MODS = 6 * KD


def lam_init(l):
    return 0.8 - 0.6 * math.exp(-0.3 * l)


def blocks_of(l, g):
    return [4 * l + 2 * g - (2 if l else 0) + t for t in range(2)]


def block_home(b):
    return (0, b) if b < 4 else (1, b - 2)


def front(l, g, ts, keys=True, queries=True):
    out = [("stat", l, g, t, 1) for t in ts] + [("norm", l, g, t, 1) for t in ts]
    names = (["qd"] if queries else []) + (["kd", "vd"] if keys else []) + (["cq"] if queries else []) + (["kv"] if keys else [])
    prior = None
    for n in names:
        if (prior, n) == ("qd", "cq"):
            out.append(("turn", l, g, prior, ts))
            prior = None
        out += [("in", l, g, n, ts, half) for half in range(2)]
        if prior and prior != "vd":
            out.append(("turn", l, g, prior, ts))
        if n in ("cq", "kv"):
            out.append(("root", l, g, n, ts))
        prior = n
    out.append(("turn", l, g, prior, ts))
    if queries:
        out += [("up", l, g, "q", ts), ("up", l, g, "r", ts)]
    if keys:
        out.append(("up", l, g, "k", ts))
    if queries:
        out.append(("turn", l, g, "q", ts))
    if keys:
        out += [("up", l, g, "v", ts), ("turn", l, g, "k", ts)]
    return out


def attention(l, g, t):
    return [("attn", l, g, t, i) for i in range(-1, MH + DH + 2)] + [("hnorm", l, g, t), ("heads", l, g, t)]


def outward(l, g, ts):
    out = []
    for n in range(2):
        out += [("gates", l, g, n, ts)] + [("out", l, g, n, ts, half) for half in range(2)]
    out += [("stat", l, g, t, 2) for t in ts]
    for t in ts:
        out += [("norm", l, g, t, 2), ("back", l, g, t)]
    return out


def pick(l, g, ts):
    out = []
    for h in range(PH + 1):
        out.append(("pick", l, g, h, ts))
        if h > 0 and len(ts) > 1:
            out.append(("also", l, g, h, ts[1:]))
    return out


def holds(s):
    return (s[0] in ("in", "out") and s[-1] == 0) or (s[0] in ("pick", "also") and s[3] % 2 == 0 and s[3] < PH)


def modulation(l, n0, n1):
    out = []
    for n in range(n0, n1):
        out.append(("ada", l, n))
        if n > n0:
            out.append(("adat", l, n - 1))
    return out + [("adat", l, n1 - 1)]


def splits_pick(s):
    return s[0] == "pick" and s[3] > 0 and len(s[4]) > 1


def mingle(first, second):
    out, at, done = [], 0, 0
    total = sum(cost(s) for s in first)
    for n, s in enumerate(first):
        out.append(s)
        done += cost(s)
        if holds(s) or splits_pick(s):
            continue
        to = done * len(second) // total
        out += second[at:to]
        at = max(at, to)
    return out + second[at:]


COST = {"stat": (45, 0), "norm": (50, 0), "in": (0, 40), "turn": (0, 10), "root": (5, 5), "up": (0, 25), "attn": (35, 0),
        "hnorm": (20, 0), "heads": (20, 0), "gates": (10, 0), "out": (0, 50), "back": (20, 0), "pick": (85, 0), "also": (80, 0),
        "ada": (50, 0), "adat": (5, 0), "mod": (5, 0)}
PER_TILE = {"in": 4, "turn": 4, "root": 4, "up": 4, "out": 4}


def cost(s):
    each, per_tile = COST[s[0]]
    return each + per_tile * (len(s[PER_TILE[s[0]]]) if s[0] in PER_TILE else 0)


def picks_of(stage):
    if stage[0] not in ("pick", "also") or stage[3] == 0:
        return []
    _, l, g, h, ts = stage
    return [blocks_of(l, g)[ts[0]] * QUADS + 4 * (h - 1)]


def weave(placed, background, stream):
    out, at, done = [], 0, 0
    total = sum(cost(s) for s in background)
    seen = set(placed)

    def step():
        nonlocal at
        out.append(stream[at])
        seen.add(stream[at])
        at += 1

    def picked(s):
        if s[0] != "quads":
            return True
        at = (s[1] * QUADS + s[2] + AHEAD) // 4 * 4
        if at >= 6 * QUADS or s[1] < 4 <= at // QUADS:
            at = s[1] * QUADS + QUADS - 4
        return any(at in picks_of(p) for p in seen)

    for n, s in enumerate(background):
        for c in needed(s):
            while c not in seen:
                step()
        out.append(s)
        done += cost(s)
        to = done * len(stream) // total
        while at < to and picked(stream[at]) and not (stream[at][0] == "close" and (s[0] in ("in", "out") and s[-1] == 0
                                                                                    or splits_pick(s))):
            step()
        seen.add(s)
    out.append(("picked", len(placed)))
    while at < len(stream):
        assert picked(stream[at]), stream[at]
        step()
    return out


def needed(s):
    if s[0] == "stat" and s[1] > 0 and s[4] == 1:
        return [("close", 2 * s[2] + s[3])]
    if s[0] == "back":
        b = blocks_of(s[1], s[2])[s[3]]
        return [("close", b - HB)] if b >= HB else []
    return []


def spans(plan):
    out = []
    for s in plan:
        if s[0] == "quads" and out and out[-1][0] == "quads" and out[-1][1] == s[1] and out[-1][3] == s[2]:
            out[-1] = ("quads", s[1], out[-1][2], s[3])
        else:
            out.append(s)
    return out


def stream_of(b, first=0, last=QUADS):
    return [("quads", b, q, q + 1) for q in range(first, last)] + ([("close", b)] if last == QUADS else [])


def make_plan():
    plan = [("consts",)]
    plan += modulation(0, 0, 4) + [("mod", 0, 1)] + front(0, CTX, BOTH)
    plan += mingle(attention(0, CTX, 0), modulation(0, 4, 10)) + [("mod", 0, 2)] + outward(0, CTX, (0,))
    first = pick(0, CTX, (0,))
    plan += first[:2]
    rest = (mingle(attention(0, CTX, 1), modulation(0, 10, 12)) + outward(0, CTX, (1,)) + pick(0, CTX, (1,)) + front(0, LAT, BOTH)
            + attention(0, LAT, 0) + attention(0, LAT, 1) + outward(0, LAT, BOTH))
    picks = pick(0, LAT, BOTH)
    plan += weave(plan, first[2:] + rest + picks[:5], stream_of(0) + stream_of(1, 0, QUADS - AHEAD))
    picks = mingle(picks[5:], modulation(1, 0, 4)) + [("mod", 1, 1)]
    fronts = mingle(front(1, CTX, BOTH, queries=False) + front(1, LAT, (0,)), modulation(1, 4, 12)) + [("mod", 1, 2)]
    plan += weave(plan, picks, stream_of(1, QUADS - AHEAD) + stream_of(2, 0, QUADS - 2 * AHEAD))
    plan += weave(plan, fronts, stream_of(2, QUADS - 2 * AHEAD) + stream_of(3))
    plan += front(1, LAT, (1,), queries=False) + attention(1, LAT, 0) + outward(1, LAT, (0,))
    first, picks = pick(1, LAT, (0,)), pick(1, LAT, (1,))
    plan += first[:2]
    rest = first[2:] + front(1, LAT, (1,), keys=False) + attention(1, LAT, 1) + outward(1, LAT, (1,)) + picks[:3]
    plan += weave(plan, rest, stream_of(4, 0, QUADS - AHEAD))
    plan += weave(plan, picks[3:], stream_of(4, QUADS - AHEAD) + [("last", 0)] + stream_of(5, 0, QUADS - 2 * AHEAD))
    plan += stream_of(5, QUADS - 2 * AHEAD) + [("last", 1)]
    at = {s: n for n, s in enumerate(plan)}
    for s in plan:
        for c in needed(s):
            assert at[c] < at[s], "a block is closed too late"
    return spans(plan)


PLAN = make_plan()


LEAD = 130


def put_off(stage, quads):
    return stage[0] in COST and not any(at <= quads[1] * QUADS + quads[3] - 1 + AHEAD for at in picks_of(stage))


def late(plan):
    out, run = [], 0
    for s in plan:
        if s[0] == "quads":
            _, b, q0, q1 = s
            first, at, jumped = ("quads", b, q0, q0 + 1), len(out), 0
            while run > 0 and jumped < LEAD and put_off(out[at - 1], first):
                at, run, jumped = at - 1, run - 1, jumped + cost(out[at - 1])
            if at == len(out):
                out.append(s)
            else:
                out.insert(at, first)
                out += [("quads", b, q0 + 1, q1)] if q1 > q0 + 1 else []
            run = 0
        else:
            out.append(s)
            run += 1
    at = {s: n for n, s in enumerate(out)}
    for s in out:
        if s[0] == "quads":
            need = s[1] * QUADS + (s[3] - 1) // 4 * 4
            assert any(at[p] < at[s] for p in out if need in picks_of(p)), "quads before their pick"
    return out


FINAL_GAIN_AFTER = sum(s[0] == "norm" for s in PLAN[:PLAN.index(("norm", DEPTH - 1, CTX, 1, 1)) + 1])


def parts_of(q0, q1):
    out, q = [], q0
    while q < q1:
        m = (q1 - q) // 4 * 4
        if q1 == QUADS:
            m = (q1 - 1 - q) // 4 * 4
        if q % 4 == 0 and q > 0 and m >= 8:
            out.append(("loop", q, q + m))
            q += m
        else:
            out.append(("one", q, q + 1))
            q += 1
    return out


def tmp_slot(name):
    return {"qd": 0, "kd": 2, "cq": 0, "kv": 2}[name]


def root_at(name, t):
    return (0 if name == "cq" else 2) + t


def slot_no(b, q, i=0):
    return b * SLOTS + q * 4 + i


class Ring:

    def __init__(self, banks):
        self.banks, self.n = banks, 0

    def next(self):
        self.n += 1
        return self.banks[(self.n - 1) % len(self.banks)], self.n


class Ticks:

    def __init__(self):
        self.n = {}

    def __call__(self, name):
        self.n[name] = self.n.get(name, 0) + 1
        return self.n[name]

    def so_far(self, name):
        return self.n.get(name, 0)


def backbone(nc, a, out):
    ctx = ExitStack()
    with ctx:
        def sb(name, shape, dt=F32):
            return ctx.enter_context(nc.sbuf_tensor(name, shape, dt))

        def sem(name):
            return ctx.enter_context(nc.semaphore(name))

        X = sb("X", [P, TILES, D])
        H2 = sb("H2", [P, HB, D])
        HT = sb("HT", [P, KD, 2 * P])
        KTM = sb("KTM", [MQ, MH, TILES * P])
        VM = sb("VM", [P, TILES, MH * MD])
        KTD = sb("KTD", [P, DH, TILES * P])
        VD = sb("VD", [P, TILES, DH * 2 * DD])
        QTM = sb("QTM", [MQ, MH, 2 * P])
        QTD = sb("QTD", [P, DH, 2 * P])
        EXPERT = sb("EXPERT", [P, RING, 2 * D])
        WT = sb("WT", [P, WSLOTS, KP, W])
        SCR = sb("SCR", [P, 4096])
        ACC = sb("ACC", [P, D])
        IDX = sb("IDX", [P, HB, SLOTS], U32)
        GATE = sb("GATE", [P, HB, SLOTS])
        FIX = sb("FIX", [P, 2, UNIT], U32)
        IDN = sb("IDN", [P, P])
        ONES = sb("ONES", [P, P])
        GD = sb("GD", [P, 4, P])
        DIAG = sb("DIAG", [P, BY_PE, P])
        COL = sb("COL", [P, 2, 2 * MODS])
        ST = sb("ST", [P, 2, KD])
        MROW = sb("MROW", [2, 2, W])
        MOD = sb("MOD", [P, DEPTH, MODS, 2])
        SKT = sb("SKT", [P, DEPTH * 2, P])
        LS = sb("LS", [P, 2 * DEPTH])
        LE = sb("LE", [P, 2 * DEPTH])
        LAM = sb("LAM", [P, DEPTH])
        SUBG = sb("SUBG", [P, DEPTH])
        ROPM = sb("ROPM", [P, 2, 2, RD])
        ROPD = sb("ROPD", [P, 2, 2, DD])
        IOTA = sb("IOTA", [P, TOPK])
        EPST = sb("EPST", [P, 1])
        KR = sb("KR", [P, 2, RD])
        SS = sb("SS", [P, 4])
        SQ = sb("SQ", [P, 4])
        RS = sb("RS", [P, 4])
        NS = sb("NS", [P, 1])
        NQ = sb("NQ", [P, 1])
        NR = sb("NR", [P, 1])
        MX = sb("MX", [P, 2, 2])
        NM = sb("NM", [P, 2, 2])
        SUM = sb("SUM", [P, 2, 2])
        INV = sb("INV", [P, 2, 2])
        SV = sb("SV", [P, 2, TOPK])
        SI = sb("SI", [P, 2, TOPK], U32)
        SIF = sb("SIF", [P, 2, TOPK])
        TS = sb("TS", [P, 2, TOPK])
        POS = sb("POS", [P, TOPK], U32)
        AB = sb("AB", [P, 2, TOPK], U32)
        ABF = sb("ABF", [P, 2, TOPK])
        PICK = sb("PICK", [P, 2, TOPK])
        TE = sb("TE", [P, 2, TOPK])
        NT = sb("NT", [P, 2])
        TSUM = sb("TSUM", [P, 2])
        TINV = sb("TINV", [P, 2])
        DOT = sb("DOT", [P, RING])
        GEL = sb("GEL", [P, 4])
        WEI = sb("WEI", [P, 4])

        SK = SCR[:, 0:DEPTH * 2 * P].rearrange("p (i n) -> p i n", n=P)
        LM = SCR[:, 512:1024].rearrange("p (l f n) -> p l f n", l=DEPTH, f=4)
        ROW = SCR[0:ROWS, 1024:1024 + P]
        BROW = SCR[0:2 * MODS, 1536:1536 + P]
        LT = SCR[:, 2048:2048 + 2 * DEPTH * DD].rearrange("p (i n) -> p i n", n=DD)
        XN = SCR[:, 0:2 * D].rearrange("p (t n) -> p t n", t=2)
        ROT = SCR[:, 0:W]
        TMP = SCR[:, D:D + 4 * W].rearrange("p (s n) -> p s n", s=4)
        ASM = SCR[:, D:4096].rearrange("p (s h n) -> p s h n", s=4, h=MH)
        PR = SCR[:, 0:2048].rearrange("p (r c n) -> p r c n", r=2, c=2)
        PT = SCR[:, 2048:3072].rearrange("p (r n) -> p r n", r=2)
        O = SCR[:, 3072:4096]
        YT = SCR[:, D:D + 2 * W].rearrange("p (s n) -> p s n", s=2)
        GROW = SCR[:, D + 2 * W:D + 3 * W]
        WK = SCR[:, D:D + 256].rearrange("p (c n) -> p c n", c=2)
        CAND = SCR[:, D + 256:D + 512]
        CANW = SCR[:, D + 512:D + 768]
        HOT = SCR[:, D + 1024:D + 1536].rearrange("p (c s n) -> p c s n", c=2, s=TOPK)
        QP = SCR[:, 3072:4096].rearrange("p (r c n) -> p r c n", r=2, c=2)

        banks_a = [ctx.enter_context(nc.psum_tensor(f"PA{i}", [P, W], F32)) for i in range(NA)]
        banks_b = [ctx.enter_context(nc.psum_tensor(f"PB{i}", [P, W], F32)) for i in range(NB)]
        VSUM = [ctx.enter_context(nc.psum_tensor(f"VS{i}", [P, W], F32)) for i in range(2)]

        consts_in = sem("consts_in")
        x_in = sem("x_in")
        fg_in = sem("fg_in")
        piece_in = [sem(f"piece_in{i}") for i in range(WSLOTS)]
        piece_used = sem("piece_used")
        filled_a, emptied_a = sem("filled_a"), sem("emptied_a")
        filled_b, emptied_b = sem("filled_b"), sem("emptied_b")
        cols_set = sem("cols_set")
        silu_done = sem("silu_done")
        mrow_ready = sem("mrow_ready")
        mod_ready = sem("mod_ready")
        lam_sums, lam_exps = sem("lam_sums"), sem("lam_exps")
        x_ready = [sem(f"x_ready{t}") for t in range(TILES)]
        root_ready = sem("root_ready")
        rs_ready = sem("rs_ready")
        xn_ready = sem("xn_ready")
        ss_ready, sq_ready = sem("ss_ready"), sem("sq_ready")
        tmp_ready = sem("tmp_ready")
        negmax_ready, exp_ready, mixed_ready = sem("negmax_ready"), sem("exp_ready"), sem("mixed_ready")
        o_ready = sem("o_ready")
        gd_ready = sem("gd_ready")
        top_ready, topexp_ready = sem("top_ready"), sem("topexp_ready")
        idx_ready = [sem(f"idx_ready{t}") for t in range(2)]
        landed = [sem(f"landed{j}") for j in range(RING)]
        fix_set, pool_step = sem("fix_set"), sem("pool_step")
        dots_ready, gelu_ready, wei_ready, diag_ready = (sem("dots_ready"), sem("gelu_ready"), sem("wei_ready"),
                                                          sem("diag_ready"))
        used_pe, used_dve = sem("used_pe"), sem("used_dve")
        vsum_read = sem("vsum_read")
        acc_zero = sem("acc_zero")
        y_ready, stored = sem("y_ready"), sem("stored")
        dve_step, act_step = sem("dve_step"), sem("act_step")

        block = ctx.enter_context(nc.Block())

        CONSTS = [(IDN[:, :], a["ident"]), (ROW[R_C:R_C + KD, :], a["c"].rearrange("b (k p) -> (b k) p", p=P)),
                  (ROW[R_CC:R_CC + KD, :], a["c_ctx"].rearrange("(k p) -> k p", p=P)),
                  (ROW[R_NA:R_NA + 16, :], a["norm_attn_g"].rearrange("l (k p) -> (l k) p", p=P)),
                  (ROW[R_NF:R_NF + 16, :], a["norm_ffn_g"].rearrange("l (k p) -> (l k) p", p=P)),
                  (ROW[R_QN:R_QN + 6, :], a["mla_q_norm_g"].rearrange("l (k p) -> (l k) p", p=P)),
                  (ROW[R_KN:R_KN + 4, :], a["mla_kv_norm_g"].rearrange("l (k p) -> (l k) p", p=P)),
                  (ROW[R_SN:R_SN + 2, :], a["diff_subnorm_g"]),
                  (BROW, a["b_ada"].rearrange("l (k p) -> (l k) p", p=P)),
                  (SK, a["peer_subkeys"].rearrange("l c k d -> k (l c) d")),
                  (SCR[:, 512:1024],
                   a["diff_lambda"].rearrange("l f d -> (l f d)").partition_broadcast(P)),
                  (ROPM[:, :, :, :], a["rope_mla"].rearrange("(t p) s n -> p t s n", p=P)),
                  (ROPD[:, :, :, :], a["rope_diff"].rearrange("(t p) s n -> p t s n", p=P)),
                  (IOTA[:, :], a["iota"].partition_broadcast(P))]
        CONSTS_ALL = 16 * len(CONSTS)

        def pieces(stage):
            kind, l = stage[0], (stage[1] if len(stage) > 1 else 0)
            if kind == "ada":
                w, (c0, n), ks = a["w_ada"][l], (stage[2] * W, W), (0, KD)
            elif kind == "in":
                w, (c0, n), ks = a["w_in"][l], CHUNKS[stage[3]], HALVES[stage[5]]
            elif kind == "out":
                w, (c0, n), ks = a["w_out"][l], (stage[3] * W, W), HALVES[stage[5]]
            elif kind == "pick" and stage[3] < PH and stage[3] % 2 == 0:
                w, (c0, n), ks = a["peer_wq"][l], (stage[3] * 256, W), (0, KD)
            elif kind == "up":
                name, n, k = {"q": ("mla_wq_up", MH * MD, 3), "r": ("mla_wq_rope", MH * RD, 3),
                              "k": ("mla_wk_up", MH * MD, 2), "v": ("mla_wv_up", MH * MD, 2)}[stage[3]]
                w, c0, ks = a[name][l], 0, (0, k)
            else:
                return []
            v = w.rearrange("(k p) n -> p k n", p=P)
            return [(v[:, k:min(k + KP, ks[1]), c0:c0 + n], min(k + KP, ks[1]) - k, n) for k in range(ks[0], ks[1], KP)]

        @block.sync
        def _(sp):
            for dst, src in CONSTS:
                sp.dma_start(dst, src).then_inc(consts_in, 16)
            xt = [a["ctx"][0, 0:P, :], a["ctx"][0, P:2 * P, :], a["x"][0, 0:P, :], a["x"][0, P:2 * P, :]]
            n = 0
            for stage in PLAN:
                for src, k, cols in pieces(stage):
                    if n >= WSLOTS:
                        sp.wait_ge(piece_used, n - WSLOTS + 1)
                    sp.dma_start(WT[:, n % WSLOTS, 0:k, 0:cols], src).then_inc(piece_in[n % WSLOTS], 16)
                    n += 1
                if stage == ("ada", 0, 1):
                    for t in range(TILES):
                        sp.dma_start(X[:, t, :], xt[t]).then_inc(x_in, 16)
                if stage == ("close", 4):
                    sp.wait_ge(xn_ready, FINAL_GAIN_AFTER)
                    sp.dma_start(X[:, 0, :], a["final_norm_g"].partition_broadcast(P)).then_inc(fg_in, 16)
                if stage[0] == "last":
                    t = stage[1]
                    sp.wait_ge(y_ready, t + 1)
                    sp.dma_start(out[0, t * P:(t + 1) * P, :], X[:, 2 + t, :]).then_inc(stored, 16)
            sp.wait_ge(stored, 32)

        @block.gpsimd
        def _(pool):
            def unit(b, u, par, fixed):
                n = u + b * (SLOTS // UNIT)

                def wait(s, v):
                    if not fixed:
                        pool.wait_ge(s, v)
                        pool.sem_inc(pool_step, 1)
                    elif v > 0:
                        pool.wait_ge(s, v)

                wait(used_pe, (n * 2 - 2) * BY_PE + 1)
                at = bass.ds(u * UNIT, UNIT) if not fixed else slice(u * UNIT, (u + 1) * UNIT)
                pool.tensor_copy(FIX[:, par, :], IDX[:, b % HB, at]).then_inc(fix_set, 1)
                wait(fix_set, n + 1)
                for j in range(UNIT):
                    if j % 4 < BY_PE:
                        wait(used_pe, (n * 2 - 2 + j // 4) * BY_PE + j % 4 + 1)
                    else:
                        wait(used_dve, n * 2 - 2 + j // 4 + 1)
                    pool.indirect_dma_start(
                        out=EXPERT[:, j, :], out_offset=None, in_=a["peer_uv"],
                        in_offset=bass.IndirectOffsetOnAxis(ap=FIX[:, par, j:j + 1], axis=0),
                    ).then_inc(landed[j], 16)

            for b in range(6):
                l, t = block_home(b)
                heads_before = PH * (b // 2)
                if b == 0:
                    pool.wait_ge(idx_ready[t % 2], 1)
                    for par in range(2):
                        unit(b, par, par, True)
                with pool.Fori(1 if b == 0 else 0, PH) as head:
                    pool.wait_ge(idx_ready[t % 2], head + (heads_before + 1))
                    pool.sem_inc(pool_step, 1)
                    for par in range(2):
                        unit(b, head * 2 + par, par, False)

        @block.tensor
        def _(pe):
            tick = Ticks()
            ra, rb = Ring(banks_a), Ring(banks_b)
            npiece = [0]
            owed = []

            def release():
                while owed:
                    s, n, count = owed.pop()
                    pe.wait_ge(s, n)
                    pe.sem_inc(piece_used, count)

            def fill_a():
                bank, n = ra.next()
                if n > NA:
                    pe.wait_ge(emptied_a, n - NA)
                return bank

            def fill_b():
                bank, n = rb.next()
                if n > NB:
                    pe.wait_ge(emptied_b, n - NB)
                return bank

            def piece():
                n = npiece[0]
                npiece[0] += 1
                pe.wait_ge(piece_in[n % WSLOTS], 16 * (n // WSLOTS + 1))
                return WT[:, n % WSLOTS, :, :]

            def turn_tiles(bank, srcs, rows):
                for i, s in enumerate(srcs):
                    last = nc.tensor.transpose(bank[0:rows, i * P:(i + 1) * P], s, IDN[:, :])
                return last

            def consts(_):
                pe.wait_ge(consts_in, CONSTS_ALL)
                bank = fill_a()
                nc.tensor.transpose(bank[:, 0:ROWS], ROW, IDN[0:ROWS, 0:ROWS])
                nc.tensor.transpose(bank[:, P:P + 2 * MODS], BROW, IDN[0:2 * MODS, 0:2 * MODS]).then_inc(filled_a, 1)
                bank = fill_b()
                turn_tiles(bank, [SK[:, i, :] for i in range(4)], P).then_inc(filled_b, 1)

            def ada(stage):
                _, l, n = stage
                if n == 0:
                    pe.wait_ge(silu_done, 1)
                bank = fill_b()
                for k in range(KD):
                    if k % KP == 0:
                        w = piece()
                    last = nc.tensor.matmul(bank[0:2, :], ST[:, :, k], w[:, k % KP, :], start=(k == 0), stop=(k == KD - 1))
                    if k == 0:
                        release()
                    if k % KP == KP - 1 and k < KD - 1:
                        last.then_inc(piece_used, 1)
                last.then_inc(filled_b, 1)
                owed.append((filled_b, rb.n, 1))

            def adat(stage):
                n = stage[2]
                pe.wait_ge(mrow_ready, tick("mrow"))
                bank = fill_a()
                for k in range(4):
                    last = nc.tensor.transpose(bank[:, 2 * k:2 * k + 2], MROW[:, n % 2, k * P:(k + 1) * P], IDN[0:2, 0:2])
                last.then_inc(filled_a, 1)

            def norm(stage):
                pe.wait_ge(xn_ready, tick("norm"))
                for half in range(2):
                    bank = fill_b()
                    turn_tiles(bank, [XN[:, stage[3], (4 * half + k) * P:(4 * half + k + 1) * P] for k in range(4)], P)\
                        .then_inc(filled_b, 1)
                held["ht", stage[3]] = rb.n

            def back(stage):
                t = stage[3]
                pe.wait_ge(emptied_b, held["ht", t])
                for half in range(2):
                    bank = fill_a()
                    turn_tiles(bank, [HT[:, 4 * half + k, t * P:(t + 1) * P] for k in range(4)], P).then_inc(filled_a, 1)

            def product(stage):
                kind, l, g, name, ts, half = stage
                n = CHUNKS[name][1] if kind == "in" else W
                if half == 0:
                    if kind == "out":
                        gate_rows()
                    pe.wait_ge(emptied_b, rb.n)
                    held["banks"] = [fill_a() for t in ts]
                    held["fills"] = ra.n
                for k0 in range(*HALVES[half], KP):
                    w = piece()
                    for t, bank in zip(ts, held["banks"]):
                        for k in range(k0, k0 + KP):
                            last = nc.tensor.matmul(bank[:, 0:n], HT[:, k, t * P:(t + 1) * P], w[:, k % KP, 0:n],
                                                    start=(k == 0), stop=(k == KD - 1))
                            if k == KD - 1:
                                last.then_inc(filled_a, 1)
                            elif k % KP == KP - 1 and t == ts[-1]:
                                last.then_inc(piece_used, 1)
                            if t == ts[0] and k == k0:
                                release()
                if half == 1:
                    owed.append((filled_a, held["fills"], 1))

            def gate_rows():
                pe.wait_ge(gd_ready, tick("gd"))
                bank = fill_a()
                for k in range(4):
                    last = nc.tensor.matmul(bank[:, k * P:(k + 1) * P], ONES[:, :], GD[:, k, :], start=True, stop=True)
                last.then_inc(filled_a, 1)

            def up(stage):
                _, l, g, what, ts = stage
                pe.wait_ge(emptied_b, rb.n)
                k0, kn, n = {"q": (0, 3, 512), "r": (0, 3, 256), "k": (3, 2, 512), "v": (3, 2, 512)}[what]
                banks = [fill_a() for t in ts]
                for k in range(kn):
                    if k % KP == 0:
                        w = piece()
                    for t, bank in zip(ts, banks):
                        last = nc.tensor.matmul(bank[:, 0:n], HT[:, k0 + k, t * P:(t + 1) * P], w[:, k % KP, 0:n],
                                                start=(k == 0), stop=(k == kn - 1))
                        if k == kn - 1:
                            last.then_inc(filled_a, 1)
                        elif k % KP == KP - 1 and t == ts[-1]:
                            last.then_inc(piece_used, 1)
                        if t == ts[0] and k == 0:
                            release()
                owed.append((filled_a, ra.n, 1))

            def turn(stage):
                _, l, g, what, ts = stage
                for t in ts:
                    pe.wait_ge(tmp_ready, tick("tmp"))
                    if what in ("q", "k"):
                        src = ASM[:, (2 if what == "k" else 0) + t, :, :]
                        for half in range(2):
                            bank = fill_b()
                            turn_tiles(bank, [src[:, 4 * half + h, :] for h in range(4)], MQ).then_inc(filled_b, 1)
                    else:
                        src = TMP[:, tmp_slot(what) + t, :]
                        cols = {"qd": 4, "kd": 4, "cq": 3, "kv": 2}[what]
                        bank = fill_b()
                        turn_tiles(bank, [src[:, k * P:(k + 1) * P] for k in range(cols)], P).then_inc(filled_b, 1)

            def attn(stage):
                _, l, g, t, i = stage
                keys = 2 * P if g == CTX else 4 * P
                if i == -1:
                    pe.wait_ge(emptied_b, rb.n)
                    pe.wait_ge(emptied_a, ra.n)
                if i + 1 < MH + DH:
                    h = i + 1
                    for c in range(1 if h < MH else 2):
                        bank = fill_b()
                        if h < MH:
                            q, k = QTM[:, h, t * P:(t + 1) * P], KTM[:, h, 0:keys]
                        else:
                            q = QTD[64 * c:64 * c + 64, h - MH, t * P:(t + 1) * P]
                            k = KTD[64 * c:64 * c + 64, h - MH, 0:keys]
                        nc.tensor.matmul(bank[:, 0:keys], q, k, start=True, stop=True).then_inc(filled_b, 1)
                if i >= 2:
                    h = i - 2
                    bank = fill_a()
                    pe.wait_ge(emptied_a, turned.pop(0))
                    v = VM[:, :, h * MD:(h + 1) * MD] if h < MH else VD[:, :, (h - MH) * P:(h - MH + 1) * P]
                    n = MD if h < MH else P
                    for k in range(keys // P):
                        last = nc.tensor.matmul(bank[:, 0:n], PT[:, h % 2, k * P:(k + 1) * P], v[:, k, :],
                                                start=(k == 0), stop=(k == keys // P - 1))
                    last.then_inc(filled_a, 1)
                if 1 <= i <= MH + DH:
                    h = i - 1
                    bank = fill_a()
                    if h < MH:
                        pe.wait_ge(exp_ready, tick.so_far("heads") + 1)
                    else:
                        pe.wait_ge(mixed_ready, tick("mixed"))
                    tick("heads")
                    turn_tiles(bank, [PR[:, h % 2, 0, k * P:(k + 1) * P] for k in range(keys // P)], P)\
                        .then_inc(filled_a, 1)
                    turned.append(ra.n)

            turned = []
            held = {}

            def heads(stage):
                pe.wait_ge(o_ready, tick("o"))
                for half in range(2):
                    bank = fill_b()
                    turn_tiles(bank, [O[:, (4 * half + k) * P:(4 * half + k + 1) * P] for k in range(4)], P)\
                        .then_inc(filled_b, 1)

            def pick_(stage):
                _, l, g, h, ts = stage
                if h == 0:
                    pe.wait_ge(emptied_b, rb.n)
                if h >= 1:
                    pe.wait_ge(emptied_b, held[h - 1, 1])
                    for t in ts:
                        bank = fill_a()
                        for c in range(2):
                            last = nc.tensor.matmul(bank[:, c * P:(c + 1) * P], QP[:, (h - 1) % 2, c, t * P:(t + 1) * P],
                                                    SKT[:, 2 * l + c, :], start=True, stop=True)
                        last.then_inc(filled_a, 1)
                if h < PH:
                    if h % 2 == 0:
                        release()
                        held["w"] = [piece() for k in range(0, KD, KP)]
                    mine = slice(ts[0] * P, (ts[-1] + 1) * P)
                    for c in range(2):
                        bank = fill_b()
                        for k in range(KD):
                            at = (h % 2) * 256 + c * P
                            last = nc.tensor.matmul(bank[:, mine], held["w"][k // KP][:, k % KP, at:at + P], HT[:, k, mine],
                                                    start=(k == 0), stop=(k == KD - 1))
                        last.then_inc(filled_b, 1)
                        held[h, c] = rb.n
                    if h % 2 == 1:
                        owed.append((filled_b, rb.n, KD // KP))

            def apply(no, i, j, first=False, last_one=False):
                pe.wait_ge(diag_ready, no + 1)
                for n in range(2):
                    ins = nc.tensor.matmul(VSUM[n][:, :], DIAG[:, i, :], EXPERT[:, j, D + n * W:D + (n + 1) * W],
                                           start=first, stop=last_one)
                ins.then_inc(used_pe, 1)

            def quads(stage):
                _, b, q0, q1 = stage
                release()
                for kind, v0, v1 in parts_of(q0, q1):
                    if kind == "loop":
                        with pe.Fori(v0 // 4, v1 // 4) as four:
                            for k in range(16):
                                if k % 4 < BY_PE:
                                    apply(four * (4 * BY_PE) + (b * QUADS + k // 4) * BY_PE + k % 4, k % 4, k % RING)
                    else:
                        if v0 == 0 and b > 0:
                            pe.wait_ge(vsum_read, 2 * b)
                        for i in range(BY_PE):
                            apply((b * QUADS + v0) * BY_PE + i, i, (v0 % 2) * 4 + i, first=(v0 + i == 0),
                                  last_one=(v0 == QUADS - 1 and i == BY_PE - 1))

            def close(stage):
                for n in range(2):
                    gate_rows()

            do = {"consts": consts, "ada": ada, "adat": adat, "norm": norm, "back": back, "in": product, "out": product,
                  "up": up, "turn": turn, "attn": attn, "heads": heads, "pick": pick_, "quads": quads, "close": close}
            for stage in PLAN:
                if stage[0] in do:
                    do[stage[0]](stage)

        @block.scalar
        def _(act):
            tick = Ticks()
            rb = Ring(banks_b)
            steps = [0]

            def link(ins):
                steps[0] += 1
                ins.then_inc(act_step, 1)
                act.wait_ge(act_step, steps[0])

            def from_b():
                bank, n = rb.next()
                act.wait_ge(filled_b, n)
                return bank

            def consts(_):
                bank = from_b()
                nc.scalar.copy(SKT[:, :, :].rearrange("p i n -> p (i n)"), bank[:, :]).then_inc(emptied_b, 1)
                act.wait_ge(cols_set, 1)
                nc.scalar.activation(ST[:, :, :].rearrange("p c k -> p (c k)"), COL[:, 0, 0:2 * KD], ACT.Silu)\
                    .then_inc(silu_done, 1)
                act.wait_ge(lam_sums, 2 * DEPTH)
                nc.scalar.activation(LE[:, :], LS[:, :], ACT.Exp).then_inc(lam_exps, 1)

            def ada(stage):
                bank = from_b()
                nc.scalar.copy(MROW[:, stage[2] % 2, :], bank[0:2, :]).then_inc(emptied_b, 1)
                act.wait_ge(emptied_b, rb.n)
                act.sem_inc(mrow_ready, 1)

            def mean_square(tile, place):
                link(nc.scalar.activation(place, X[:, tile, :], ACT.Square, accum_out=NS[:, :]))
                nc.scalar.activation(NQ[:, :], NS[:, :], ACT.Sqrt, scale=1.0 / D, bias=EPST[:, :]).then_inc(root_ready, 1)

            def stat(stage):
                _, l, g, t, which = stage
                tile = 2 * g + t
                if which == 1 and l == 0:
                    act.wait_ge(x_in, 16 * TILES)
                else:
                    act.wait_ge(x_ready[tile], 2 * l + (which == 2))
                mean_square(tile, XN[:, t, :])
                act.wait_ge(rs_ready, tick("norm"))
                nc.scalar.activation(XN[:, t, :], X[:, tile, :], ACT.Copy, scale=NR[:, :]).then_inc(xn_ready, 1)

            def norm(stage):
                _, l, g, t, which = stage
                act.wait_ge(mod_ready, 2 * l + which)
                at = (1 if which == 1 else 4) * KD
                m = 1 - g
                for half in range(2):
                    bank = from_b()
                    for k in range(4):
                        j = at + 4 * half + k
                        last = nc.scalar.activation(HT[:, 4 * half + k, t * P:(t + 1) * P], bank[:, k * P:(k + 1) * P],
                                                    ACT.Identity, scale=MOD[:, l, j, m:m + 1],
                                                    bias=MOD[:, l, j - KD, m:m + 1])
                    last.then_inc(emptied_b, 1)

            def root(stage):
                _, l, g, what, ts = stage
                act.wait_ge(ss_ready, tick("ss"))
                at = slice(root_at(what, ts[0]), root_at(what, ts[-1]) + 1)
                nc.scalar.activation(SQ[:, at], SS[:, at], ACT.Sqrt, scale=1.0 / (QR if what == "cq" else KVR),
                                     bias=EPST[:, :]).then_inc(sq_ready, 1)

            def turn(stage):
                _, l, g, what, ts = stage
                for t in ts:
                    keys = slice((2 * g + t) * P, (2 * g + t + 1) * P)
                    mine = slice(t * P, (t + 1) * P)
                    if what in ("q", "k"):
                        dst, at = (QTM, mine) if what == "q" else (KTM, keys)
                        for half in range(2):
                            bank = from_b()
                            nc.scalar.copy(dst[:, 4 * half:4 * half + 4, at],
                                           bank[0:MQ, :].rearrange("p (h n) -> p h n", h=4)).then_inc(emptied_b, 1)
                    elif what in ("qd", "kd"):
                        dst, at = (QTD, mine) if what == "qd" else (KTD, keys)
                        bank = from_b()
                        nc.scalar.copy(dst[:, :, at], bank[:, :].rearrange("p (h n) -> p h n", h=4))\
                            .then_inc(emptied_b, 1)
                    else:
                        k0, kn, r = (0, 3, R_QN + 3 * l) if what == "cq" else (3, 2, R_KN + 2 * l)
                        bank = from_b()
                        for k in range(kn):
                            last = nc.scalar.activation(HT[:, k0 + k, mine], bank[:, k * P:(k + 1) * P], ACT.Copy,
                                                        scale=COL[:, 0, r + k:r + k + 1])
                        last.then_inc(emptied_b, 1)

            def attn(stage):
                _, l, g, t, i = stage
                keys = 2 * P if g == CTX else 4 * P
                h = i + 1
                if h < MH + DH:
                    act.wait_ge(negmax_ready, tick("negmax"))
                    for c in range(1 if h < MH else 2):
                        bank = from_b()
                        ins = nc.scalar.activation(PR[:, h % 2, c, 0:keys], bank[:, 0:keys], ACT.Exp,
                                                   bias=NM[:, h % 2, c:c + 1], scale=SC_M if h < MH else SC_D,
                                                   accum_out=SUM[:, h % 2, c:c + 1])
                        ins.then_inc(emptied_b, 1)
                    act.wait_ge(emptied_b, rb.n)
                    act.sem_inc(exp_ready, 1)

            def hnorm(stage):
                act.wait_ge(ss_ready, tick("ss"))
                nc.scalar.activation(SQ[:, :], SS[:, :], ACT.Sqrt, scale=1.0 / P, bias=EPST[:, :]).then_inc(sq_ready, 1)

            def heads(stage):
                _, l, g, t = stage
                for half in range(2):
                    bank = from_b()
                    src = bank[:, :].rearrange("p (h n) -> p h n", h=4)
                    dst = HT[:, 4 * half:4 * half + 4, t * P:(t + 1) * P]
                    if half == 0:
                        nc.scalar.copy(dst, src).then_inc(emptied_b, 1)
                    else:
                        nc.scalar.activation(dst, src, ACT.Copy, scale=SUBG[:, l:l + 1]).then_inc(emptied_b, 1)

            def pick_(stage):
                _, l, g, h, ts = stage
                if h >= 1:
                    gate_exps(ts[0])
                if h < PH:
                    for c in range(2):
                        bank = from_b()
                        nc.scalar.copy(QP[:, h % 2, c, ts[0] * P:(ts[-1] + 1) * P], bank[:, ts[0] * P:(ts[-1] + 1) * P])\
                            .then_inc(emptied_b, 1)

            def also(stage):
                gate_exps(stage[4][0])

            def gate_exps(t):
                act.wait_ge(top_ready, tick("top"))
                nc.scalar.activation(TE[:, t, :], TS[:, t, :], ACT.Exp, bias=NT[:, t:t + 1],
                                     accum_out=TSUM[:, t:t + 1]).then_inc(topexp_ready, 1)

            def weigh(no, mine, i, j, gate):
                one = slice(i, i + 1)
                act.wait_ge(dots_ready, no + 1)
                nc.scalar.activation(GEL[:, one], DOT[:, j:j + 1], ACT.Gelu).then_inc(gelu_ready, 1)
                act.wait_ge(gelu_ready, no + 1)
                nc.scalar.activation(WEI[:, one], GEL[:, one], ACT.Copy, scale=gate).then_inc(wei_ready, 1)
                if i < BY_PE:
                    act.wait_ge(wei_ready, no + 1)
                    if not isinstance(mine, int) or mine >= BY_PE:
                        act.wait_ge(used_pe, mine - BY_PE + 1)
                    nc.scalar.activation(DIAG[:, i, :], IDN[:, :], ACT.Copy, scale=WEI[:, one]).then_inc(diag_ready, 1)

            def quads(stage):
                _, b, q0, q1 = stage
                for kind, v0, v1 in parts_of(q0, q1):
                    if kind == "loop":
                        with act.Fori(v0 // 4, v1 // 4) as four:
                            for i in range(16):
                                weigh(four * 16 + (b * SLOTS + i), four * (4 * BY_PE) + (b * QUADS + i // 4) * BY_PE + i % 4,
                                      i % 4, i % RING, GATE[:, b % HB, bass.ds(four * 16 + i, 1)])
                    else:
                        for i in range(4):
                            weigh(slot_no(b, v0, i), (b * QUADS + v0) * BY_PE + i, i, slot_no(b, v0, i) % RING,
                                  GATE[:, b % HB, v0 * 4 + i:v0 * 4 + i + 1])

            def last_(stage):
                t = stage[1]
                act.wait_ge(x_ready[2 + t], 4)
                tick("norm")
                mean_square(2 + t, XN[:, t, :])

            do = {"consts": consts, "ada": ada, "stat": stat, "norm": norm, "root": root, "turn": turn, "attn": attn,
                  "hnorm": hnorm, "heads": heads, "pick": pick_, "also": also, "quads": quads, "last": last_}
            for stage in late(PLAN):
                if stage[0] in do:
                    do[stage[0]](stage)

        @block.vector
        def _(dve):
            tick = Ticks()
            ra, rb = Ring(banks_a), Ring(banks_b)
            steps = [0]

            def link(ins):
                steps[0] += 1
                ins.then_inc(dve_step, 1)
                dve.wait_ge(dve_step, steps[0])

            def from_a():
                bank, n = ra.next()
                dve.wait_ge(filled_a, n)
                return bank

            def tt(o, x, y, op):
                return nc.vector.tensor_tensor(o, x, y, op)

            def consts(_):
                nc.vector.memset(EPST[:, :], EPS)
                nc.vector.memset(ONES[:, :], 1.0)
                dve.wait_ge(consts_in, CONSTS_ALL)
                bank = from_a()
                nc.vector.tensor_copy(COL[:, 0, 0:ROWS], bank[:, 0:ROWS]).then_inc(cols_set, 1)
                dve.wait_ge(cols_set, 1)
                link(nc.vector.tensor_copy(COL[:, 1, :], bank[:, P:P + 2 * MODS]))
                nc.vector.tensor_scalar(SUBG[:, 0:1], COL[:, 0, R_SN:R_SN + 1], 1.0 - lam_init(0), None, ALU.mult)
                nc.vector.tensor_scalar(SUBG[:, 1:2], COL[:, 0, R_SN + 1:R_SN + 2], 1.0 - lam_init(1), None, ALU.mult)\
                    .then_inc(emptied_a, 1)
                rb.next()
                for l in range(DEPTH):
                    for i in range(2):
                        nc.vector.tensor_tensor_reduce(out=LT[:, 2 * l + i, :], in0=LM[:, l, 2 * i, :], in1=LM[:, l, 2 * i + 1, :],
                                                       scale=1.0, scalar=0.0, op0=ALU.mult, op1=ALU.add,
                                                       accum_out=LS[:, 2 * l + i:2 * l + i + 1]).then_inc(lam_sums, 1)
                dve.wait_ge(lam_exps, 1)
                for l in range(DEPTH):
                    link(tt(LAM[:, l:l + 1], LE[:, 2 * l:2 * l + 1], LE[:, 2 * l + 1:2 * l + 2], ALU.subtract))
                    link(nc.vector.tensor_scalar(LAM[:, l:l + 1], LAM[:, l:l + 1], lam_init(l), None, ALU.add))

            def ada(stage):
                rb.next()

            def adat(stage):
                _, l, n = stage
                bank = from_a()
                tt(MOD[:, l, 4 * n:4 * n + 4, :], bank[:, 0:8].rearrange("p (k c) -> p k c", c=2),
                   COL[:, 1, l * MODS + 4 * n:l * MODS + 4 * n + 4].unsqueeze(2).to_broadcast([P, 4, 2]),
                   ALU.add).then_inc(emptied_a, 1)

            def mod(stage):
                _, l, which = stage
                dve.wait_ge(emptied_a, ra.n)
                at, r = (KD, R_NA) if which == 1 else (4 * KD, R_NF)
                m = MOD[:, l, at:at + KD, :]
                link(nc.vector.tensor_scalar(m, m, 1.0, None, ALU.add))
                tt(m, m, COL[:, 0, r + l * KD:r + (l + 1) * KD].unsqueeze(2).to_broadcast([P, KD, 2]), ALU.mult)\
                    .then_inc(mod_ready, 1)
                dve.wait_ge(mod_ready, 2 * l + which)

            def invert():
                dve.wait_ge(root_ready, tick("norm"))
                nc.vector.reciprocal(NR[:, :], NQ[:, :]).then_inc(rs_ready, 1)
                dve.wait_ge(rs_ready, tick.so_far("norm"))

            def stat(stage):
                invert()

            def norm(stage):
                rb.next()
                rb.next()

            def back(stage):
                _, l, g, t = stage
                b = blocks_of(l, g)[t]
                for half in range(2):
                    bank = from_a()
                    nc.vector.tensor_copy(H2[:, b % HB, half * W:(half + 1) * W], bank[:, :]).then_inc(emptied_a, 1)
                dve.wait_ge(emptied_a, ra.n)

            def rotate(dst, src, table, heads, width):
                def table_at(s, odd):
                    v = table[:, s, :].rearrange("p (n two) -> p n two", two=2)[:, :, odd]
                    return v.unsqueeze(1).to_broadcast([P, heads, width // 2])

                r = ROT[:, 0:heads * width].rearrange("p (h n) -> p h n", h=heads)
                r2 = r.rearrange("p h (n two) -> p h n two", two=2)
                s2 = src.rearrange("p h (n two) -> p h n two", two=2)
                tt(r2[:, :, :, 0], s2[:, :, :, 1], table_at(1, 0), ALU.mult)
                tt(r2[:, :, :, 1], s2[:, :, :, 0], table_at(1, 1), ALU.mult)
                link(tt(dst, src, table[:, 0, :].unsqueeze(1).to_broadcast([P, heads, width]), ALU.mult))
                return tt(dst, dst, r, ALU.add)

            def roots(at):
                dve.wait_ge(sq_ready, tick("sq"))
                link(nc.vector.reciprocal(RS[:, at], SQ[:, at]))

            def in_(stage):
                _, l, g, what, ts, half = stage
                if half == 0:
                    return
                if what in pend_free and pend_free[what] in turned:
                    dve.wait_ge(filled_b, turned[pend_free[what]])
                for t in ts:
                    bank = from_a()
                    tile = 2 * g + t
                    tmp = TMP[:, (0 if what == "vd" else tmp_slot(what)) + t, :]
                    if what == "vd":
                        nc.vector.tensor_copy(VD[:, tile, :], bank[:, :]).then_inc(emptied_a, 1)
                    elif what in ("qd", "kd"):
                        if g == LAT:
                            link(rotate(tmp.rearrange("p (h n) -> p h n", n=DD),
                                        bank[:, :].rearrange("p (h n) -> p h n", n=DD), ROPD[:, t, :, :], 2 * DH, DD))
                            free_a()
                            dve.sem_inc(tmp_ready, 1)
                        else:
                            link(nc.vector.tensor_copy(tmp, bank[:, :]))
                            free_a()
                            dve.sem_inc(tmp_ready, 1)
                    else:
                        n = QR if what == "cq" else KVR
                        link(nc.vector.tensor_copy(tmp[:, 0:n], bank[:, 0:n]))
                        if what == "kv":
                            kr = KR[:, t, :].unsqueeze(1)
                            src = bank[:, n:n + RD].unsqueeze(1)
                            if g == LAT:
                                link(rotate(kr, src, ROPM[:, t, :, :], 1, RD))
                            else:
                                link(nc.vector.tensor_copy(kr, src))
                        free_a()
                        ins = nc.vector.tensor_tensor_reduce(out=ROT[:, 0:n], in0=tmp[:, 0:n], in1=tmp[:, 0:n], scale=1.0,
                                                             scalar=0.0, op0=ALU.mult, op1=ALU.add,
                                                             accum_out=SS[:, root_at(what, t):root_at(what, t) + 1])
                        if t != ts[-1]:
                            link(ins)
                        else:
                            ins.then_inc(ss_ready, 1)
                            dve.wait_ge(ss_ready, tick("ss"))

            def free_a():
                dve.sem_inc(emptied_a, 1)

            pend_free = {"cq": "qd", "kv": "kd"}
            turned = {}

            def root(stage):
                _, l, g, what, ts = stage
                roots(slice(root_at(what, ts[0]), root_at(what, ts[-1]) + 1))
                for t in ts:
                    tmp = TMP[:, tmp_slot(what) + t, 0:QR if what == "cq" else KVR]
                    nc.vector.tensor_scalar(tmp, tmp, RS[:, root_at(what, t):root_at(what, t) + 1], None, ALU.mult)\
                        .then_inc(tmp_ready, 1)

            def turn(stage):
                _, l, g, what, ts = stage
                for t in range(len(ts) * (2 if what in ("q", "k") else 1)):
                    rb.next()
                turned[what] = rb.n
                if what in ("q", "k"):
                    turned.clear()

            def up(stage):
                _, l, g, what, ts = stage
                if what in ("q", "k", "v"):
                    for t in ts:
                        bank = from_a()
                        tile = 2 * g + t
                        if what == "v":
                            nc.vector.tensor_copy(VM[:, tile, :], bank[:, :]).then_inc(emptied_a, 1)
                            continue
                        asm = ASM[:, (2 if what == "k" else 0) + t, :, :]
                        nc.vector.tensor_copy(asm[:, :, 0:MD], bank[:, :].rearrange("p (h n) -> p h n", n=MD))\
                            .then_inc(emptied_a, 1)
                        if what == "k":
                            nc.vector.tensor_copy(asm[:, :, MD:MQ], KR[:, t, :].unsqueeze(1).to_broadcast([P, MH, RD]))\
                                .then_inc(tmp_ready, 1)
                else:
                    for t in ts:
                        bank = from_a()
                        asm = ASM[:, t, :, :]
                        src = bank[:, 0:MH * RD].rearrange("p (h n) -> p h n", n=RD)
                        if g == LAT:
                            link(rotate(asm[:, :, MD:MQ], src, ROPM[:, t, :, :], MH, RD))
                        else:
                            link(nc.vector.tensor_copy(asm[:, :, MD:MQ], src))
                        free_a()
                        dve.sem_inc(tmp_ready, 1)

            def attn(stage):
                _, l, g, t, i = stage
                keys = 2 * P if g == CTX else 4 * P
                h = i + 1
                if h < MH + DH:
                    maps = 1 if h < MH else 2
                    for c in range(maps):
                        bank, n = rb.next()
                        dve.wait_ge(filled_b, n)
                        ins = nc.vector.reduce_max(MX[:, h % 2, c:c + 1], bank[:, 0:keys], AX_X)
                    steps[0] += 1
                    ins.then_inc(dve_step, 1)
                if i >= 2:
                    done = i - 2
                    bank = from_a()
                    if done < MH:
                        nc.vector.tensor_scalar(O[:, done * MD:(done + 1) * MD], bank[:, 0:MD], INV[:, done % 2, 0:1], None,
                                                ALU.mult).then_inc(emptied_a, 1)
                    else:
                        at = MH * MD + (done - MH) * P
                        nc.vector.tensor_copy(O[:, at:at + P], bank[:, 0:P]).then_inc(emptied_a, 1)
                if 1 <= i <= MH + DH:
                    bank = from_a()
                    nc.vector.tensor_copy(PT[:, (i - 1) % 2, 0:keys], bank[:, 0:keys]).then_inc(emptied_a, 1)
                if h < MH + DH:
                    dve.wait_ge(dve_step, steps[0])
                    nc.vector.tensor_scalar(NM[:, h % 2, 0:maps], MX[:, h % 2, 0:maps], -(SC_M if h < MH else SC_D), None,
                                            ALU.mult).then_inc(negmax_ready, 1)
                if 0 <= i < MH + DH:
                    maps = 1 if i < MH else 2
                    dve.wait_ge(exp_ready, tick("exp"))
                    dve.wait_ge(emptied_a, ra.n)
                    link(nc.vector.reciprocal(INV[:, i % 2, 0:maps], SUM[:, i % 2, 0:maps]))
                    if i >= MH:
                        link(tt(INV[:, i % 2, 1:2], INV[:, i % 2, 1:2], LAM[:, l:l + 1], ALU.mult))
                        p0, p1 = PR[:, i % 2, 0, 0:keys], PR[:, i % 2, 1, 0:keys]
                        link(nc.vector.tensor_scalar(p1, p1, INV[:, i % 2, 1:2], None, ALU.mult))
                        nc.vector.scalar_tensor_tensor(out=p0, in0=p0, scalar=INV[:, i % 2, 0:1], in1=p1, op0=ALU.mult,
                                                       op1=ALU.subtract).then_inc(mixed_ready, 1)

            def hnorm(stage):
                dve.wait_ge(emptied_a, ra.n)
                od = O[:, MH * MD:D].rearrange("p (h n) -> p h n", h=DH)
                sq = PT[:, 0, :].rearrange("p (h n) -> p h n", h=DH)
                link(tt(sq, od, od, ALU.mult))
                nc.vector.tensor_reduce(SS[:, :], sq, AX_X, ALU.add).then_inc(ss_ready, 1)
                tick("ss")
                roots(slice(0, 4))
                tt(od, od, RS[:, :].unsqueeze(2).to_broadcast([P, DH, P]), ALU.mult).then_inc(o_ready, 1)

            def heads(stage):
                rb.next()
                rb.next()

            def diagonals(l, g, which, n):
                at = (2 if which == 1 else 5) * KD + 4 * n
                m = 1 - g
                tt(GD[:, :, :], IDN[:, :].unsqueeze(1).to_broadcast([P, 4, P]),
                   MOD[:, l, at:at + 4, m:m + 1].to_broadcast([P, 4, P]), ALU.mult).then_inc(gd_ready, 1)

            def gates(stage):
                _, l, g, n, ts = stage
                diagonals(l, g, 1, n)

            def out_(stage):
                _, l, g, n, ts, half = stage
                if half == 0:
                    return
                bank = from_a()
                nc.vector.tensor_copy(GROW, bank[:, :]).then_inc(emptied_a, 1)
                dve.wait_ge(emptied_a, ra.n)
                for t in ts:
                    bank = from_a()
                    x = X[:, 2 * g + t, n * W:(n + 1) * W]
                    tt(YT[:, t, :], bank[:, :], GROW, ALU.mult).then_inc(emptied_a, 1)
                    dve.wait_ge(emptied_a, ra.n)
                    ins = tt(x, x, YT[:, t, :], ALU.add)
                    if n == 1:
                        ins.then_inc(x_ready[2 * g + t], 1)

            def pick_(stage):
                _, l, g, h, ts = stage
                if h < PH:
                    rb.next()
                    rb.next()
                if h == 0:
                    return
                top(ts[0])
                experts(l, g, h - 1, ts[0])

            def also(stage):
                _, l, g, h, ts = stage
                top(ts[0])
                experts(l, g, h - 1, ts[0])

            def mark(ins):
                steps[0] += 1
                ins.then_inc(dve_step, 1)
                return steps[0]

            def after(n):
                dve.wait_ge(dve_step, n)

            def top(t):
                bank = from_a()
                s = [bank[:, c * P:(c + 1) * P] for c in range(2)]
                low = [mark(nc.vector.max(SV[:, c, 0:8], s[c])) for c in range(2)]
                rest = []
                for c in range(2):
                    after(low[c])
                    rest.append(mark(nc.vector.match_replace(WK[:, c, :], SV[:, c, 0:8], s[c], LOWEST)))
                high = []
                for c in range(2):
                    nc.vector.max_index(SI[:, c, 0:8], SV[:, c, 0:8], s[c])
                for c in range(2):
                    after(rest[c])
                    high.append(mark(nc.vector.max(SV[:, c, 8:16], WK[:, c, :])))
                for c in range(2):
                    after(high[c])
                    found = mark(nc.vector.max_index(SI[:, c, 8:16], SV[:, c, 8:16], WK[:, c, :]))
                free_a()
                sums = mark(tt(CAND.rearrange("p (i j) -> p i j", i=TOPK), SV[:, 0, :].unsqueeze(2).to_broadcast([P, TOPK, TOPK]),
                               SV[:, 1, :].unsqueeze(1).to_broadcast([P, TOPK, TOPK]), ALU.add))
                after(found)
                nc.vector.tensor_copy(SIF[:, :, :], SI[:, :, :])
                after(sums)
                low = mark(nc.vector.max(TS[:, t, 0:8], CAND))
                after(low)
                rest = mark(nc.vector.match_replace(CANW, TS[:, t, 0:8], CAND, LOWEST))
                nc.vector.max_index(POS[:, 0:8], TS[:, t, 0:8], CAND)
                after(rest)
                high = mark(nc.vector.max(TS[:, t, 8:16], CANW))
                nc.vector.tensor_scalar(NT[:, t:t + 1], TS[:, t, 0:1], -1.0, None, ALU.mult).then_inc(top_ready, 1)
                after(high)
                after(mark(nc.vector.max_index(POS[:, 8:16], TS[:, t, 8:16], CANW)))

            def experts(l, g, h, t):
                b = blocks_of(l, g)[t]
                nc.vector.tensor_scalar(AB[:, 0, :], POS[:, :], 4, None, ALU.logical_shift_right)
                after(mark(nc.vector.tensor_scalar(AB[:, 1, :], POS[:, :], 15, None, ALU.bitwise_and)))
                after(mark(nc.vector.tensor_copy(ABF[:, :, :], AB[:, :, :])))
                hot = [mark(tt(HOT[:, c], ABF[:, c, :].unsqueeze(2).to_broadcast([P, TOPK, TOPK]),
                               IOTA[:, :].unsqueeze(1).to_broadcast([P, TOPK, TOPK]), ALU.is_equal)) for c in range(2)]
                keys = []
                for c in range(2):
                    after(hot[c])
                    keys.append(mark(tt(HOT[:, c], HOT[:, c], SIF[:, c, :].unsqueeze(1).to_broadcast([P, TOPK, TOPK]), ALU.mult)))
                for c in range(2):
                    after(keys[c])
                    found = mark(nc.vector.tensor_reduce(PICK[:, c, :], HOT[:, c], AX_X, ALU.add))
                dve.wait_ge(topexp_ready, tick("topexp"))
                inverted = mark(nc.vector.reciprocal(TINV[:, t:t + 1], TSUM[:, t:t + 1]))
                after(found)
                at = slice(h * TOPK, (h + 1) * TOPK)
                both = mark(nc.vector.scalar_tensor_tensor(out=PICK[:, 0, :], in0=PICK[:, 0, :], scalar=float(NK),
                                                           in1=PICK[:, 1, :], op0=ALU.mult, op1=ALU.add))
                after(inverted)
                nc.vector.tensor_scalar(GATE[:, b % HB, at], TE[:, t, :], TINV[:, t:t + 1], None, ALU.mult)
                after(both)
                nc.vector.tensor_scalar(IDX[:, b % HB, at], PICK[:, 0, :], float(l * NK * NK), None, ALU.add)\
                    .then_inc(idx_ready[t], 1)
                dve.wait_ge(idx_ready[t], 8 * (b // 2) + h + 1)

            def dot(b, j, landing):
                dve.wait_ge(landed[j], landing * 16)
                nc.vector.tensor_tensor_reduce(out=EXPERT[:, j, 0:D], in0=EXPERT[:, j, 0:D], in1=H2[:, b % HB, :],
                                               scale=1.0, scalar=0.0, op0=ALU.mult, op1=ALU.add,
                                               accum_out=DOT[:, j:j + 1]).then_inc(dots_ready, 1)

            def apply(no, quad, j):
                dve.wait_ge(wei_ready, no + 1)
                if not isinstance(quad, int) or quad > 0:
                    dve.wait_ge(used_dve, quad)
                nc.vector.scalar_tensor_tensor(out=ACC[:, :], in0=EXPERT[:, j, D:2 * D], scalar=WEI[:, BY_PE:BY_PE + 1],
                                               in1=ACC[:, :], op0=ALU.mult, op1=ALU.add).then_inc(used_dve, 1)

            def quads(stage):
                _, b, q0, q1 = stage
                for kind, v0, v1 in parts_of(q0, q1):
                    if kind == "loop":
                        with dve.Fori(v0 // 4, v1 // 4) as four:
                            for i in range(16):
                                dot(b, i % RING, four * 2 + ((b * SLOTS + i) // RING + 1))
                                if i % 4 == 0:
                                    apply(four * 16 + (b * SLOTS + i - 1), four * 4 + (b * QUADS + i // 4 - 1), (i - 1) % RING)
                    else:
                        if v0 == 0:
                            nc.vector.memset(ACC[:, :], 0.0).then_inc(acc_zero, 1)
                            dve.wait_ge(acc_zero, b + 1)
                        for i in range(4):
                            no = slot_no(b, v0, i)
                            dot(b, no % RING, no // RING + 1)
                            if i == 0 and v0 > 0:
                                apply(no - 1, b * QUADS + v0 - 1, (no - 1) % RING)

            def close(stage):
                b = stage[1]
                l, tile = block_home(b)
                no = slot_no(b + 1, 0)
                apply(no - 1, (b + 1) * QUADS - 1, RING - 1)
                diagonals(l, tile // 2, 2, 0)
                dve.wait_ge(used_dve, (b + 1) * QUADS)
                dve.wait_ge(used_pe, (b + 1) * QUADS * BY_PE)
                for n in range(2):
                    half = slice(n * W, (n + 1) * W)
                    if n == 1:
                        diagonals(l, tile // 2, 2, n)
                    tt(ACC[:, half], ACC[:, half], VSUM[n][:, :], ALU.add).then_inc(vsum_read, 1)
                    rows = from_a()
                    dve.wait_ge(vsum_read, 2 * b + n + 1)
                    link(tt(ACC[:, half], ACC[:, half], rows[:, :], ALU.mult))
                    free_a()
                    x = X[:, tile, half]
                    ins = tt(x, x, ACC[:, half], ALU.add)
                    if n == 1:
                        ins.then_inc(x_ready[tile], 1)
                        dve.wait_ge(x_ready[tile], 2 * l + 2)

            def last_(stage):
                t = stage[1]
                invert()
                dve.wait_ge(fg_in, 16)
                x = X[:, 2 + t, :]
                nc.vector.scalar_tensor_tensor(out=x, in0=x, scalar=NR[:, :], in1=X[:, 0, :], op0=ALU.mult,
                                               op1=ALU.mult).then_inc(y_ready, 1)

            do = {"consts": consts, "ada": ada, "adat": adat, "mod": mod, "stat": stat, "norm": norm, "back": back,
                  "in": in_, "out": out_, "gates": gates, "up": up, "root": root, "turn": turn, "attn": attn,
                  "hnorm": hnorm, "heads": heads, "pick": pick_, "also": also, "quads": quads, "close": close, "last": last_}
            for stage in late(PLAN):
                if stage[0] in do:
                    do[stage[0]](stage)


_INS = ["x", "c", "ctx", "c_ctx", "norm_attn_g", "norm_ffn_g", "w_ada", "b_ada", "w_in", "mla_q_norm_g", "mla_wq_up",
        "mla_wq_rope", "mla_kv_norm_g", "mla_wk_up", "mla_wv_up", "diff_lambda", "diff_subnorm_g", "w_out", "peer_wq",
        "peer_subkeys", "final_norm_g"]


def rope_table(np, width, seq=256, grid=64, base=10000.0):
    quarter = width // 4
    freq = (np.float32(base) ** (-np.arange(quarter, dtype=np.float32) / np.float32(quarter))).astype(np.float32)
    row = np.repeat(np.arange(seq // grid, dtype=np.float32), grid)
    col = np.tile(np.arange(grid, dtype=np.float32), seq // grid)
    ang = np.concatenate([row[:, None] * freq, col[:, None] * freq], axis=-1)
    cos = np.repeat(np.cos(ang), 2, axis=-1)
    sin = np.repeat(np.sin(ang), 2, axis=-1) * np.tile(np.array([-1.0, 1.0], np.float32), width // 2)
    return np.stack([cos, sin], axis=1).astype(np.float32)


def kernel(**inputs):
    import numpy as np
    import concourse.bacc as bacc
    from concourse.bass_utils import run_bass_kernel_spmd

    nc = bacc.Bacc("TRN2", target_bir_lowering=False, num_devices=1)
    host = {n: np.asarray(inputs[n]) for n in _INS}
    u, v = np.asarray(inputs["peer_u"]), np.asarray(inputs["peer_v"])
    host["peer_uv"] = np.concatenate([u, v], axis=-1).reshape(-1, u.shape[-1] + v.shape[-1])
    host["ident"] = np.eye(P, dtype=np.float32)
    host["iota"] = np.arange(TOPK, dtype=np.float32)
    host["rope_mla"] = rope_table(np, RD)
    host["rope_diff"] = rope_table(np, DD)
    arrays, aps = {}, {}
    for name, arr in host.items():
        arr = np.ascontiguousarray(arr)
        arrays[f"in_{name}"] = arr
        aps[name] = nc.dram_tensor(f"in_{name}", arr.shape, mybir.dt.from_np(arr.dtype), kind="ExternalInput").ap()
    out = nc.dram_tensor("out_y", (1, 256, D), F32, kind="ExternalOutput").ap()
    backbone(nc, aps, out)
    got = run_bass_kernel_spmd(nc, [arrays], core_ids=[0])
    return got.results[0]["out_y"]
```
